# Optimizing a Trainium2 kernel written in Bass

```python
import jax, jax.numpy as jnp
from jax import lax
import numpy as np

D_MODEL = 1024
BATCH = 1
SEQ = 512
DEPTH = 4

CHUNK = 64
N_MIXERS = 3
RMS_EPS = 1e-6
ROPE_THETA = 500000.0
NEG_INF = -1e30
D_FF = 4 * D_MODEL

MLA_HEADS = 8
MLA_NOPE = 128
MLA_ROPE = 64
MLA_V = 128
MLA_Q_LORA = 384
MLA_KV_LORA = 256
Q_BLOCK = 128

LRU_WIDTH = D_MODEL
LRU_BLOCKS = 8
LRU_BLOCK = LRU_WIDTH // LRU_BLOCKS
CONV_WIDTH = 4
LRU_C = 8.0

SWA_Q_HEADS = 16
SWA_KV_HEADS = 4
SWA_HEAD_DIM = D_MODEL // SWA_Q_HEADS
SWA_ROT_DIM = SWA_HEAD_DIM // 4
SWA_WINDOW = 128
SWA_WIN_CHUNKS = SWA_WINDOW // CHUNK

N_MLA_LAYERS = (DEPTH + 2) // 3
N_LRU_LAYERS = (DEPTH + 1) // 3
N_SWA_LAYERS = DEPTH // 3

kernel_name = 'hybrid_mla_rglru_swa_chunk_causal'

def _rmsnorm(x, g):
    xf = x.astype(jnp.float32)
    y = xf * lax.rsqrt(jnp.mean(xf * xf, axis=-1, keepdims=True) + RMS_EPS)
    return (y * g.astype(jnp.float32)).astype(x.dtype)

def _rope(x, positions, rot_dim):
    half = rot_dim // 2
    inv_freq = jnp.float32(ROPE_THETA) ** (-jnp.arange(half, dtype=jnp.float32) / half)
    ang = positions.astype(jnp.float32)[:, :, None, None] * inv_freq
    cos, sin = jnp.cos(ang), jnp.sin(ang)
    xr = x[..., :rot_dim].astype(jnp.float32)
    x1, x2 = xr[..., :half], xr[..., half:]
    rot = jnp.concatenate([x1 * cos - x2 * sin, x2 * cos + x1 * sin], axis=-1).astype(x.dtype)
    return jnp.concatenate([rot, x[..., rot_dim:]], axis=-1)

def _mla(h, positions, w_in, q_norm, kv_norm, w_uq, w_ukv, w_o):
    B, S, _ = h.shape
    proj = h @ w_in
    c_q, c_kv, k_rope = jnp.split(proj, [MLA_Q_LORA, MLA_Q_LORA + MLA_KV_LORA], axis=-1)
    q = (_rmsnorm(c_q, q_norm) @ w_uq).reshape(B, S, MLA_HEADS, MLA_NOPE + MLA_ROPE)
    q_nope = q[..., :MLA_NOPE]
    q_rope = _rope(q[..., MLA_NOPE:], positions, MLA_ROPE)
    kv = (_rmsnorm(c_kv, kv_norm) @ w_ukv).reshape(B, S, MLA_HEADS, MLA_NOPE + MLA_V)
    k_nope, v = kv[..., :MLA_NOPE], kv[..., MLA_NOPE:]
    k_rope = _rope(k_rope[:, :, None, :], positions, MLA_ROPE)[:, :, 0, :]
    scale = (MLA_NOPE + MLA_ROPE) ** -0.5
    chunk_id = jnp.arange(S) // CHUNK
    outs = []
    for s0 in range(0, S, Q_BLOCK):
        e = s0 + Q_BLOCK
        s = (jnp.einsum('bqhd,bkhd->bhqk', q_nope[:, s0:e], k_nope[:, :e])
             + jnp.einsum('bqhd,bkd->bhqk', q_rope[:, s0:e], k_rope[:, :e])).astype(jnp.float32) * scale
        mask = chunk_id[s0:e, None] >= chunk_id[None, :e]
        p = jax.nn.softmax(jnp.where(mask, s, NEG_INF), axis=-1).astype(v.dtype)
        outs.append(jnp.einsum('bhqk,bkhd->bqhd', p, v[:, :e]))
    o = jnp.concatenate(outs, axis=1).reshape(B, S, MLA_HEADS * MLA_V)
    return o @ w_o

def _lin_rec_combine(left, right):
    a1, b1 = left
    a2, b2 = right
    return (a1 * a2, a2 * b1 + b2)

def _rglru_block(h, w_in, conv_w, conv_b, w_rgate, b_rgate, w_igate, b_igate, lam, w_out):
    B, S, _ = h.shape
    gate_branch, xb = jnp.split(h @ w_in, 2, axis=-1)
    xp = jnp.pad(xb, ((0, 0), (CONV_WIDTH - 1, 0), (0, 0)))
    xc = conv_b
    for k in range(CONV_WIDTH):
        xc = xc + xp[:, k:k + S] * conv_w[k]
    xblk = xc.reshape(B, S, LRU_BLOCKS, LRU_BLOCK)
    r = jax.nn.sigmoid(jnp.einsum('bsnk,nkj->bsnj', xblk, w_rgate).reshape(B, S, LRU_WIDTH) + b_rgate)
    ig = jax.nn.sigmoid(jnp.einsum('bsnk,nkj->bsnj', xblk, w_igate).reshape(B, S, LRU_WIDTH) + b_igate)
    log_a = -LRU_C * r.astype(jnp.float32) * jax.nn.softplus(-lam.astype(jnp.float32))
    a = jnp.exp(log_a)
    u = jnp.sqrt(-jnp.expm1(2.0 * log_a)) * (ig * xc).astype(jnp.float32)
    _, hs = lax.associative_scan(_lin_rec_combine, (a, u), axis=1)
    y = jax.nn.gelu(gate_branch) * hs.astype(h.dtype)
    return y @ w_out

def _window_chunks(t):
    nc = t.shape[1]
    parts = [jnp.pad(t, ((0, 0), (o, 0), (0, 0), (0, 0), (0, 0)))[:, :nc]
             for o in range(SWA_WIN_CHUNKS - 1, -1, -1)]
    return jnp.concatenate(parts, axis=2)

def _swa(h, positions, w_in, b_in, sinks, w_o, b_o):
    B, S, _ = h.shape
    nc = S // CHUNK
    G = SWA_Q_HEADS // SWA_KV_HEADS
    qkv = h @ w_in + b_in
    q, k, v = jnp.split(qkv, [SWA_Q_HEADS * SWA_HEAD_DIM, (SWA_Q_HEADS + SWA_KV_HEADS) * SWA_HEAD_DIM], axis=-1)
    q = _rope(q.reshape(B, S, SWA_Q_HEADS, SWA_HEAD_DIM), positions, SWA_ROT_DIM)
    k = _rope(k.reshape(B, S, SWA_KV_HEADS, SWA_HEAD_DIM), positions, SWA_ROT_DIM)
    q = q.reshape(B, nc, CHUNK, SWA_KV_HEADS, G, SWA_HEAD_DIM)
    kw = _window_chunks(k.reshape(B, nc, CHUNK, SWA_KV_HEADS, SWA_HEAD_DIM))
    vw = _window_chunks(v.reshape(B, nc, CHUNK, SWA_KV_HEADS, SWA_HEAD_DIM))
    s = jnp.einsum('bcqhgd,bckhd->bchgqk', q, kw).astype(jnp.float32) * (SWA_HEAD_DIM ** -0.5)
    offs = jnp.repeat(jnp.arange(SWA_WIN_CHUNKS - 1, -1, -1), CHUNK)
    valid = jnp.arange(nc)[:, None] >= offs[None, :]
    s = jnp.where(valid[None, :, None, None, None, :], s, NEG_INF)
    sink = jnp.broadcast_to(sinks.astype(jnp.float32).reshape(SWA_KV_HEADS, G)[None, None, :, :, None, None],
                            s.shape[:-1] + (1,))
    p = jax.nn.softmax(jnp.concatenate([s, sink], axis=-1), axis=-1)[..., :-1].astype(vw.dtype)
    o = jnp.einsum('bchgqk,bckhd->bcqhgd', p, vw).reshape(B, S, SWA_Q_HEADS * SWA_HEAD_DIM)
    return o @ w_o + b_o

def _squared_relu_mlp(h, w1, w2):
    return jnp.square(jax.nn.relu(h @ w1)) @ w2

def setup_inputs(seed: int = 0) -> dict:
    key = jax.random.key(seed)
    ks = jax.random.split(key, 28)
    f32 = jnp.float32

    def nrm(k, shape, fan_in):
        return jax.random.normal(k, shape, f32) * (fan_in ** -0.5)

    def gain(k, shape):
        return 1.0 + 0.02 * jax.random.normal(k, shape, f32)

    def small(k, shape):
        return 0.01 * jax.random.normal(k, shape, f32)

    x = jax.random.normal(ks[0], (BATCH, SEQ, D_MODEL), f32)
    offset = jax.random.randint(ks[1], (BATCH, 1), 0, 128, dtype=jnp.int32) * CHUNK
    positions = (offset + jnp.arange(SEQ, dtype=jnp.int32)[None, :]).astype(jnp.int32)

    u = jax.random.uniform(ks[19], (N_LRU_LAYERS, LRU_WIDTH), f32, minval=0.9, maxval=0.999)
    pa = u ** (1.0 / LRU_C)
    lru_lambda = jnp.log(pa) - jnp.log1p(-pa)

    return {
        'x': x,
        'positions': positions,
        'norm_mix': gain(ks[2], (DEPTH, D_MODEL)),
        'norm_mlp': gain(ks[3], (DEPTH, D_MODEL)),
        'norm_final': gain(ks[4], (D_MODEL,)),
        'mla_w_in': nrm(ks[5], (N_MLA_LAYERS, D_MODEL, MLA_Q_LORA + MLA_KV_LORA + MLA_ROPE), D_MODEL),
        'mla_q_norm': gain(ks[6], (N_MLA_LAYERS, MLA_Q_LORA)),
        'mla_kv_norm': gain(ks[7], (N_MLA_LAYERS, MLA_KV_LORA)),
        'mla_w_uq': nrm(ks[8], (N_MLA_LAYERS, MLA_Q_LORA, MLA_HEADS * (MLA_NOPE + MLA_ROPE)), MLA_Q_LORA),
        'mla_w_ukv': nrm(ks[9], (N_MLA_LAYERS, MLA_KV_LORA, MLA_HEADS * (MLA_NOPE + MLA_V)), MLA_KV_LORA),
        'mla_w_o': nrm(ks[10], (N_MLA_LAYERS, MLA_HEADS * MLA_V, D_MODEL), MLA_HEADS * MLA_V),
        'lru_w_in': nrm(ks[11], (N_LRU_LAYERS, D_MODEL, 2 * LRU_WIDTH), D_MODEL),
        'lru_conv_w': nrm(ks[12], (N_LRU_LAYERS, CONV_WIDTH, LRU_WIDTH), CONV_WIDTH),
        'lru_conv_b': small(ks[13], (N_LRU_LAYERS, LRU_WIDTH)),
        'lru_w_rgate': nrm(ks[14], (N_LRU_LAYERS, LRU_BLOCKS, LRU_BLOCK, LRU_BLOCK), LRU_BLOCK),
        'lru_b_rgate': small(ks[15], (N_LRU_LAYERS, LRU_WIDTH)),
        'lru_w_igate': nrm(ks[16], (N_LRU_LAYERS, LRU_BLOCKS, LRU_BLOCK, LRU_BLOCK), LRU_BLOCK),
        'lru_b_igate': small(ks[17], (N_LRU_LAYERS, LRU_WIDTH)),
        'lru_lambda': lru_lambda,
        'lru_w_out': nrm(ks[18], (N_LRU_LAYERS, LRU_WIDTH, D_MODEL), LRU_WIDTH),
        'swa_w_in': nrm(ks[20], (N_SWA_LAYERS, D_MODEL, (SWA_Q_HEADS + 2 * SWA_KV_HEADS) * SWA_HEAD_DIM), D_MODEL),
        'swa_b_in': small(ks[21], (N_SWA_LAYERS, (SWA_Q_HEADS + 2 * SWA_KV_HEADS) * SWA_HEAD_DIM)),
        'swa_sinks': 0.5 * jax.random.normal(ks[22], (N_SWA_LAYERS, SWA_Q_HEADS), f32),
        'swa_w_o': nrm(ks[23], (N_SWA_LAYERS, SWA_Q_HEADS * SWA_HEAD_DIM, D_MODEL), SWA_Q_HEADS * SWA_HEAD_DIM),
        'swa_b_o': small(ks[24], (N_SWA_LAYERS, D_MODEL)),
        'mlp_w1': nrm(ks[25], (DEPTH, D_MODEL, D_FF), D_MODEL),
        'mlp_w2': nrm(ks[26], (DEPTH, D_FF, D_MODEL), D_FF),
    }

def reference(x, positions, norm_mix, norm_mlp, norm_final,
              mla_w_in, mla_q_norm, mla_kv_norm, mla_w_uq, mla_w_ukv, mla_w_o,
              lru_w_in, lru_conv_w, lru_conv_b, lru_w_rgate, lru_b_rgate, lru_w_igate, lru_b_igate,
              lru_lambda, lru_w_out,
              swa_w_in, swa_b_in, swa_sinks, swa_w_o, swa_b_o,
              mlp_w1, mlp_w2):
    for i in range(DEPTH):
        kind, j = i % N_MIXERS, i // N_MIXERS
        h = _rmsnorm(x, norm_mix[i])
        if kind == 0:
            y = _mla(h, positions, mla_w_in[j], mla_q_norm[j], mla_kv_norm[j],
                     mla_w_uq[j], mla_w_ukv[j], mla_w_o[j])
        elif kind == 1:
            y = _rglru_block(h, lru_w_in[j], lru_conv_w[j], lru_conv_b[j], lru_w_rgate[j], lru_b_rgate[j],
                             lru_w_igate[j], lru_b_igate[j], lru_lambda[j], lru_w_out[j])
        else:
            y = _swa(h, positions, swa_w_in[j], swa_b_in[j], swa_sinks[j], swa_w_o[j], swa_b_o[j])
        x = x + y
        x = x + _squared_relu_mlp(_rmsnorm(x, norm_mlp[i]), mlp_w1[i], mlp_w2[i])
    return _rmsnorm(x, norm_final)


_drawn_inputs = setup_inputs


def setup_inputs(seed=0):
    import zlib

    import numpy as np

    out = dict(_drawn_inputs(seed))
    spreads = {}
    factors = {'norm_mix': 2.971,
     'norm_final': 8.149,
     'mla_q_norm': 8.0,
     'mla_kv_norm': 8.0,
     'lru_conv_b': 2.93,
     'lru_b_rgate': 8.0,
     'lru_b_igate': 8.0,
     'swa_b_in': 8.0,
     'swa_sinks': 64.0,
     'swa_b_o': 8.0}
    for name, (base, spread) in spreads.items():
        noise = np.random.default_rng([zlib.crc32(name.encode()), seed]).standard_normal(out[name].shape)
        drawn = base * np.exp(spread * noise) if base else spread * noise
        out[name] = __import__('jax').numpy.asarray(drawn.astype(out[name].dtype))
    for name, factor in factors.items():
        out[name] = (out[name] * factor).astype(out[name].dtype)
    return out
```

```python
from contextlib import ExitStack

import numpy as np

import concourse.bass as bass
from concourse import mybir

ALU = mybir.AluOpType
ACT = mybir.ActivationFunctionType
AX = mybir.AxisListType
F32 = mybir.dt.float32
F32R = mybir.dt.float32r
I32 = mybir.dt.int32

P = 128
D = 1024
T = 512
KC = D // P
F = 4 * D
DEPTH = 4
EPS = 1e-6
NEG = -1e30
CHUNK = 64
TURN = 6.283185
ROUND = 1.5 * 2.0 ** 23

H = 8
NOPE = 128
ROPE = 64
VD = 128
QL = 384
KVL = 256
SCALE = (NOPE + ROPE) ** -0.5
HALF_HEADS = H // 2
QB = T // P

SW_H = 16
SW_G = 4
SW_D = 64

SLOTS = 4
UNIT = 3 * 2 * (NOPE + ROPE)
PAIR = 2 * T
SLICE = 1024
SLICES = F // SLICE
SLICE_UNITS = 16
ARENA = 18 * T + 3 * 1280

S_OFF = {3: 0, 2: 512, 1: 896, 0: 1152}
T_OFF = {0: 0, 1: 512, 2: 896, 3: 1152}
ATT = 1280
W_ATT = 1792

COLS = {}
_at = 0
for _name, _n in (("norm_mix", DEPTH * 8), ("norm_mlp", DEPTH * 8), ("norm_final", 8),
                  ("q_norm", 2 * 3), ("kv_norm", 2 * 2), ("conv_w", 4 * 8), ("conv_b", 8),
                  ("b_rgate", 8), ("b_igate", 8), ("lambda", 8), ("swa_b_qk", 10), ("swa_b_o", 8)):
    COLS[_name] = _at
    _at += _n
NCOLS = _at

C_IDENT, C_PERM = 0, 128
C_MASK = C_PERM + 2 * 128
C_FREQ = C_MASK + 256
C_SIGN = C_FREQ + 2
NCONST = C_SIGN + 2


def rope_constants():
    c = np.zeros((P, NCONST), np.float32)
    c[:, C_IDENT:C_IDENT + P] = np.eye(P)
    for n, (rows, rot) in enumerate(((ROPE, ROPE), (SW_D, SW_D // 4))):
        half = rot // 2
        e = (-np.arange(half, dtype=np.float32) / np.float32(half)).astype(np.float64)
        freq = np.power(500000.0, e).astype(np.float32)
        for p in range(P):
            r = p % rows
            if r < rot:
                other = p + half if r < half else p - half
                c[other, C_PERM + n * P + p] = 1.0
                c[p, C_FREQ + n] = freq[r % half]
                c[p, C_SIGN + n] = -TURN if r < half else TURN
    c[:CHUNK, C_MASK:C_MASK + CHUNK] = NEG
    c[:CHUNK, C_MASK + 3 * CHUNK:C_MASK + 4 * CHUNK] = NEG
    c[CHUNK:, C_MASK:C_MASK + 2 * CHUNK] = NEG
    return c


def turn_parts():
    pi = 31415926535897932384626433832795028841971693993751
    left = (10 ** 49 << 199) // pi
    parts = []
    for bits in (14, 26, 38, 50):
        unit = 1 << (200 - bits)
        part = (left + unit // 2) // unit
        parts.append(part / (1 << bits))
        left -= part * unit
    return parts


def weight_units():
    u = []

    def mlp(i):
        for s in range(SLICES):
            for g in range(2):
                u.extend(("w1", i, s, g, kp, PAIR) for kp in range(4))
            for g in range(2):
                u.extend(("w2", i, s, g, kp, PAIR) for kp in range(4))

    def square(name, j, groups, first=0):
        for g in range(groups):
            u.extend((name, j, first + g, kp, PAIR) for kp in range(4))

    def mla(j):
        square("mla_in", j, 1)
        u.extend(("mla_in_tail", j, kq, 4 * 256) for kq in range(2))
        for half in range(2):
            u.extend(("mla_uq", j, 2 * half + n, UNIT) for n in range(2))
            u.extend(("mla_ukv", j, 2 * half + n, PAIR) for n in range(2))
        square("mla_o", j, 2)

    def lru():
        square("lru_in", 0, 2, 2)
        u.append(("lru_gates", 0, PAIR))
        square("lru_in", 0, 1, 0)
        u.append(("lru_gates", 1, PAIR))
        square("lru_in", 0, 1, 1)
        square("lru_out", 0, 2)

    def swa():
        square("swa_in", 0, 3)
        square("swa_o", 0, 2)

    for kind, i in PHASES:
        {"mla": lambda: mla(i), "lru": lru, "swa": swa, "mlp": lambda: mlp(i), "final": lambda: None}[kind]()
    return u


LOADS = {"lru_gates": 2, "mla_in_tail": 2, "mla_uq": 4}


PHASE_UNITS = {"mla": 22, "lru": 26, "swa": 20, "mlp": SLICES * SLICE_UNITS, "final": 0}
PHASES = [("mla", 0), ("mlp", 0), ("lru", 0), ("mlp", 1), ("swa", 0), ("mlp", 2), ("mla", 1), ("mlp", 3),
          ("final", 0)]

PER_TURN = {"unit": SLICE_UNITS, "tensor_unit": SLICE_UNITS, "psum_done": 4, "squared": 4, "u_hi": 4, "u_ready": 4,
            "x_ready": 4}
PER_TURN |= {f"area{a}": 2 for a in range(4)} | {f"loaded{s}": 16 * SLICE_UNITS // SLOTS for s in range(SLOTS)}


class Counts:

    def __init__(self):
        self.n = {}
        self.turn = None

    def at(self, name, more=0):
        v = self.n.get(name, 0) + more
        return v if self.turn is None else self.turn * PER_TURN[name] + v

    def add(self, name, k=1):
        self.n[name] = self.n.get(name, 0) + k

    def now(self, name):
        return self.n.get(name, 0)

    def begin(self, turn):
        self.turn, self.before = turn, dict(self.n)

    def end(self, turns):
        for name, v in self.n.items():
            rose = v - self.before.get(name, 0)
            assert rose in (0, PER_TURN.get(name, 0)), (name, rose)
            self.n[name] = v + rose * (turns - 1)
        self.turn = None


def need(eng, sem, value):
    if not isinstance(value, int) or value > 0:
        eng.wait_ge(sem, value)


def trunk(nc, A):
    units = weight_units()
    starts = [sum(PHASE_UNITS[k] for k, _ in PHASES[:n]) for n in range(len(PHASES))]
    assert len(units) == sum(PHASE_UNITS[k] for k, _ in PHASES)
    with ExitStack() as ctx:
        def sb(name, shape, dt=F32):
            return ctx.enter_context(nc.sbuf_tensor(name, shape, dt))

        def sem(name):
            return ctx.enter_context(nc.semaphore(name))

        psum = ctx.enter_context(nc.psum_tensor("psum", [P, 4 * PAIR], F32))

        x = sb("x", [P, KC * T])
        h_hi, h_lo = sb("h_hi", [P, KC * T], F32R), sb("h_lo", [P, KC * T], F32R)
        u_hi, u_lo = sb("u_hi", [P, KC * T], F32R), sb("u_lo", [P, KC * T], F32R)
        w_raw = sb("w_raw", [P, SLOTS * UNIT])
        w_hi, w_lo = sb("w_hi", [P, SLOTS * UNIT], F32R), sb("w_lo", [P, SLOTS * UNIT], F32R)
        ssq = sb("ssq", [P, T])
        sq = sb("sq", [P, 2 * T])
        var = sb("var", [P, T])
        root = sb("root", [P, T])
        rstd, rstd2 = sb("rstd", [P, T]), sb("rstd2", [P, T])
        cos, sin = sb("cos", [P, T]), sb("sin", [P, T])
        const = sb("const_sb", [P, NCONST])
        ones = sb("ones", [P, P])
        cols = sb("cols_sb", [P, NCOLS])
        small = sb("small", [P, 100])
        arena = sb("arena", [P, ARENA])

        def cut(*sizes):
            out, at = {}, 0
            for name, n in sizes:
                out[name] = arena[:, at:at + n]
                at += n
            assert at <= ARENA, at
            return out

        mlp_m = cut(("relu", 2 * PAIR), ("scaled", 2 * PAIR))
        mla_m = cut(("qn", 4 * T), ("qr", 2 * T), ("kn", 4 * T), ("kr", T), ("v", 4 * T), ("rq", T), ("rkv", T),
                    ("rope", T), ("pt", ATT), ("p", 2 * ATT))
        lru_m = cut(("gate", 8 * T), ("xc", 8 * T), ("r", 2 * T), ("i", 2 * T), ("t", 2 * T), ("xpad", 2 * (T + 3)))
        swa_m = cut(("q", 8 * T), ("kd", 4 * T), ("v", 4 * 256), ("bv", 256), ("sinks", 16), ("pt", W_ATT),
                    ("p", 2 * W_ATT))
        tab_m = cut(("before", 18 * T), ("pos", T), ("ang", T), ("head", T), ("rest", T), ("n", T), ("sum", T))

        eps_col = small[:, 96:97]
        sp4, spm8 = small[:, 72:80], small[:, 80:88]
        rotary = [0, 1, 0]
        tables = {("mla", 0): 2, ("swa", 0): 4, ("mla", 1): 6}

        ident = const[:, C_IDENT:C_IDENT + P]

        def col(name, k=0, n=1):
            return cols[:, COLS[name] + k:COLS[name] + k + n]

        def chunk(t, k, n=1):
            return t[:, k * T:(k + n) * T]

        def area(a):
            return psum[:, a * PAIR:(a + 1) * PAIR]

        def bank(a, b=0):
            return psum[:, a * PAIR + b * T:a * PAIR + (b + 1) * T]

        def twice(t):
            return t.unsqueeze(1).to_broadcast([P, 2, T])

        def two(t):
            return t.rearrange("p (a n) -> p a n", a=2)

        x_loaded = [sem(f"x_loaded{i}") for i in range(4)]
        cols_loaded = sem("cols_loaded")
        const_loaded = sem("const_loaded")
        pos_loaded = sem("pos_loaded")
        extra_loaded = sem("extra_loaded")
        w_loaded = [sem(f"w_loaded{i}") for i in range(SLOTS)]
        w_hi_done = sem("w_hi_done")
        w_ready = sem("w_ready")
        unit_done = sem("unit_done")
        psum_done = sem("psum_done")
        area_free = [sem(f"area_free{a}") for a in range(5)]
        ones_set = sem("ones_set")
        h_hi_done = sem("h_hi_done")
        h_ready = sem("h_ready")
        squares = sem("squares")
        squares_added = sem("squares_added")
        var_ready = sem("var_ready")
        root_done = sem("root_done")
        inv_done = sem("inv_done")
        pool_step = sem("pool_step")
        rstd_ready = sem("rstd_ready")
        squared = sem("squared")
        u_hi_done = sem("u_hi_done")
        u_ready = sem("u_ready")
        x_ready = sem("x_ready")
        vec_step = sem("vec_step")
        act_step = sem("act_step")
        turns_ready = sem("turns_ready")
        table_done = sem("table_done")
        rows_ready = sem("rows_ready")
        mixed = sem("mixed")
        nmax_ready = sem("nmax_ready")
        exp_done = sem("exp_done")
        p_ready = sem("p_ready")
        o_hi_done = sem("o_hi_done")
        y_done = sem("y_done")
        gate_done = sem("gate_done")
        lam_exp = sem("lam_exp")
        softplus = sem("softplus")
        xc_done = sem("xc_done")
        xc_hi_done = sem("xc_hi_done")
        xc_ready = sem("xc_ready")
        tanh_done = sem("tanh_done")
        decay_in = sem("decay_in")
        decay_used = sem("decay_used")
        roots = sem("roots")
        scanned = sem("scanned")
        biased = sem("biased")
        out_ready = sem("out_ready")
        stored = sem("stored")

        HI = [chunk(h_hi, k) for k in range(KC)]
        LO = [chunk(h_lo, k) for k in range(KC)]
        UHI = [chunk(u_hi, k) for k in range(KC)]
        ULO = [chunk(u_lo, k) for k in range(KC)]
        OHI, OLO = HI[4:] + UHI[4:], LO[4:] + ULO[4:]

        def gains(n):
            if n + 1 < len(PHASES) - 1:
                layer, is_mlp = divmod(n + 1, 2)
                return lambda k: ("norm_mlp" if is_mlp else "norm_mix", 8 * layer + k)

        def before_rotary(n):
            return n + 1 < len(PHASES) and PHASES[n + 1][0] in ("swa", "mla")

        block = ctx.enter_context(nc.Block())
        TURNS = SLICES - 1
        passed = []
        jobs = {}

        @block.sync
        def _(sp):
            c = Counts()

            def source(u, turn):
                kind = u[0]
                rows = "(a p) n -> p a n"
                if kind == "w1":
                    _, i, s, g, kp, _ = u
                    at = s * SLICE + g * T if turn is None else turn * SLICE + (s * SLICE + g * T)
                    return A["mlp_w1"][i, kp * 256:(kp + 1) * 256, bass.ds(at, T)].rearrange(rows, p=P)
                if kind == "w2":
                    _, i, s, g, kp, _ = u
                    at = s * SLICE + kp * 256 if turn is None else turn * SLICE + (s * SLICE + kp * 256)
                    return A["mlp_w2"][i, bass.ds(at, 256), g * T:(g + 1) * T].rearrange(rows, p=P)
                if kind == "mla_ukv":
                    return A["mla_w_ukv"][u[1], :, u[2] * 512:(u[2] + 1) * 512].rearrange(rows, p=P)
                name = {"mla_in": "mla_w_in", "mla_o": "mla_w_o", "lru_in": "lru_w_in", "lru_out": "lru_w_out",
                        "swa_in": "swa_w_in", "swa_o": "swa_w_o"}[kind]
                _, j, g, kp, _ = u
                return A[name][j, kp * 256:(kp + 1) * 256, g * T:(g + 1) * T].rearrange(rows, p=P)

            def load(u, turn=None):
                slot = c.now("unit") % SLOTS
                need(sp, w_ready, c.at("unit", 1 - SLOTS))
                to = w_raw[:, slot * UNIT:slot * UNIT + u[-1]]
                if u[0] == "lru_gates":
                    for n, name in enumerate(("lru_w_rgate", "lru_w_igate")):
                        sp.dma_start(to[:, n * T:(n + 1) * T].rearrange("p (b n) -> p b n", b=4),
                                     A[name][0, 4 * u[1]:4 * u[1] + 4].rearrange("b p n -> p b n")
                                     ).then_inc(w_loaded[slot], 16)
                elif u[0] == "mla_in_tail":
                    src = A["mla_w_in"][u[1], u[2] * 512:(u[2] + 1) * 512, T:T + 192].rearrange(
                        "(a p) n -> p a n", p=P)
                    to = to.rearrange("p (a n) -> p a n", a=4)
                    sp.dma_start(to[:, :, 0:192], src).then_inc(w_loaded[slot], 16)
                    sp.dma_start(to[:, :, 192:256], src[:, :, 128:192]).then_inc(w_loaded[slot], 16)
                elif u[0] == "mla_uq":
                    to = to.rearrange("p (a n) -> p a n", a=3)
                    for hh in range(2):
                        first = (2 * u[2] + hh) * (NOPE + ROPE)
                        src = A["mla_w_uq"][u[1], :, first:first + NOPE + ROPE].rearrange("(a p) n -> p a n", p=P)
                        sp.dma_start(to[:, :, hh * NOPE:(hh + 1) * NOPE], src[:, :, 0:NOPE]
                                     ).then_inc(w_loaded[slot], 16)
                        at = 2 * NOPE + hh * ROPE
                        sp.dma_start(to[:, :, at:at + ROPE], src[:, :, NOPE:]).then_inc(w_loaded[slot], 16)
                else:
                    src = source(u, turn)
                    sp.dma_start(to.rearrange("p (a n) -> p a n", n=src.shape[2]), src).then_inc(w_loaded[slot], 16)
                c.add("unit")

            def load_positions():
                sp.dma_start(tab_m["pos"].bitcast(I32), A["positions"].partition_broadcast(P)).then_inc(pos_loaded, 16)

            sp.dma_start(cols[:, :], A["cols"]).then_inc(cols_loaded, 16)
            for p in range(4):
                sp.dma_start(two(chunk(x, 2 * p, 2)), A["x"][p * 256:(p + 1) * 256, :].rearrange(
                    "(a p) n -> p a n", p=P)).then_inc(x_loaded[p], 16)
                load(units[p])
                if p == 0:
                    sp.dma_start(const[:, :], A["const"]).then_inc(const_loaded, 16)
                    load_positions()
            for n, (kind, i) in enumerate(PHASES):
                start = starts[n]
                if kind == "swa":
                    sp.dma_start(swa_m["bv"], A["swa_bv"].partition_broadcast(P)).then_inc(extra_loaded, 16)
                    sp.dma_start(swa_m["sinks"], A["swa_sinks"].partition_broadcast(P)).then_inc(extra_loaded, 16)
                if kind == "mlp":
                    for u in units[max(start, c.now("unit")):start + 8]:
                        load(u)
                    with sp.Fori(0, TURNS) as turn:
                        c.begin(turn)
                        for u in units[start + 8:start + 8 + SLICE_UNITS]:
                            load(u, turn)
                        c.end(TURNS)
                    if before_rotary(n):
                        load_positions()
                    for u in units[start + 56:start + 64]:
                        load(u)
                else:
                    for u in units[max(start, c.now("unit")):start + PHASE_UNITS[kind]]:
                        load(u)
            for k in range(KC):
                sp.wait_ge(out_ready, k + 1)
                sp.dma_start(A["out"][k * P:(k + 1) * P, :], chunk(arena, k)).then_inc(stored, 16)
            sp.wait_ge(stored, 16 * KC)

        @block.tensor
        def _(pe):
            c = Counts()

            def claim(a):
                need(pe, area_free[a], c.at(f"area{a}"))
                c.add(f"area{a}")

            def unit(at=0, n=PAIR):
                slot = (c.now("tensor_unit") + at) % SLOTS
                return w_hi[:, slot * UNIT:slot * UNIT + n], w_lo[:, slot * UNIT:slot * UNIT + n]

            def next_unit_ready(at=0):
                pe.wait_ge(w_ready, c.at("tensor_unit", at + 1))

            def product(out, stat, mov, start, stop, skip=False):
                nc.tensor.matmul(out, stat[0], mov[0], start=start, stop=False, skip_group_check=skip)
                nc.tensor.matmul(out, stat[0], mov[1], start=False, stop=False, skip_group_check=skip)
                return nc.tensor.matmul(out, stat[1], mov[0], start=False, stop=stop, skip_group_check=skip)

            def column_sums(a, source, b=0):
                return nc.tensor.matmul(bank(a, b), ones[:, :], source, start=True, stop=True)

            def square_group(areas, hi, lo, ready, before_unit=None):
                claim(areas[0])
                claim(areas[1])
                outs = [bank(areas[0], 0), bank(areas[0], 1), bank(areas[1], 0), bank(areas[1], 1)]
                for kp in range(4):
                    if before_unit and kp in before_unit:
                        before_unit[kp]()
                    next_unit_ready()
                    ready(kp)
                    wh, wl = unit()

                    def tile(kk, m):
                        at = slice(kk * T + m * P, kk * T + (m + 1) * P)
                        k = 2 * kp + kk
                        return product(outs[m], (wh[:, at], wl[:, at]), (hi[k], lo[k]), k == 0, k == KC - 1)

                    if kp < 3:
                        order = [(kk, m) for kk in range(2) for m in range(4)]
                    else:
                        order = [(kk, m) for half in range(2) for kk in range(2) for m in (2 * half, 2 * half + 1)]
                    for n, (kk, m) in enumerate(order):
                        mm = tile(kk, m)
                        if kp == 3 and n == 3:
                            mm.then_inc(psum_done, 1)
                            c.add("psum_done")
                    mm.then_inc(unit_done, 1)
                    c.add("tensor_unit")

            def h_chunks(kp):
                pe.wait_ge(h_ready, c.now("h") + 2 * kp + 2)

            def anything(kp):
                pass

            def norm_sums(a):
                def run():
                    claim(a)
                    pe.wait_ge(squares_added, c.now("squares_added") + 7)
                    column_sums(a, ssq[:, :]).then_inc(psum_done, 1)
                    c.add("psum_done")
                    c.add("squares_added", 7)
                return run

            def up(g, before_unit=None, h_wait=anything):
                square_group((0, 1) if g == 0 else (2, 3), HI, LO, h_wait, before_unit)

            def down(g):
                def ready(kp):
                    pe.wait_ge(u_ready, c.at("u_ready", kp + 1))
                square_group((0, 1) if g == 0 else (2, 3), UHI, ULO, ready if g == 0 else anything)
                if g == 1:
                    c.add("u_ready", 4)

            def mlp():
                up(0, {3: norm_sums(2)}, h_chunks)
                c.add("h", 8)
                with pe.Fori(0, TURNS) as turn:
                    c.begin(turn)
                    up(1)
                    down(0)
                    down(1)
                    up(0)
                    c.end(TURNS)
                up(1)
                down(0)
                down(1)

            def swap_rows(out, which, source):
                perm = const[:, C_PERM + which * P:C_PERM + (which + 1) * P]
                return nc.tensor.matmul(out, perm, source, start=True, stop=True)

            def token_columns(a, rows):
                claim(a)
                for t in range(QB):
                    mm = nc.tensor.matmul(bank(a)[:, t:t + 1], rows[0:1, t * P:(t + 1) * P], ones[0:1, 0:1],
                                          start=True, stop=True)
                mm.then_inc(psum_done, 1)
                c.add("psum_done")

            def mla(j):
                square_group((0, 1), HI, LO, h_chunks, {3: norm_sums(2)})
                c.add("h", 8)
                claim(3)
                for kq in range(2):
                    next_unit_ready()
                    wh, wl = (w.rearrange("p (a n) -> p a n", n=256) for w in unit())
                    for kk in range(4):
                        k = 4 * kq + kk
                        for b in range(2):
                            st = (wh[:, kk, b * P:(b + 1) * P], wl[:, kk, b * P:(b + 1) * P])
                            mm = product(bank(3, b), st, (HI[k], LO[k]), k == 0, k == KC - 1)
                    mm.then_inc(unit_done, 1)
                    c.add("tensor_unit")
                claim(2)
                pe.wait_ge(squares_added, c.now("squares_added") + 2)
                column_sums(2, mla_m["rq"]).then_inc(psum_done, 1)
                c.add("psum_done")

                def queries(areas):
                    next_unit_ready()
                    wh, wl = (w.rearrange("p (k n) -> p k n", k=3) for w in unit(0, UNIT))
                    claim(areas[0])
                    for hh in range(2):
                        for k in range(3):
                            at = slice(hh * NOPE, (hh + 1) * NOPE)
                            mm = product(bank(areas[0], hh), (wh[:, k, at], wl[:, k, at]),
                                         (UHI[k], ULO[k]), k == 0, k == 2)
                    mm.then_inc(psum_done, 1)
                    c.add("psum_done")
                    claim(areas[1])
                    for k in range(3):
                        mm = product(bank(areas[1]), (wh[:, k, 2 * NOPE:], wl[:, k, 2 * NOPE:]),
                                     (UHI[k], ULO[k]), k == 0, k == 2)
                    mm.then_inc(unit_done, 1)
                    c.add("tensor_unit")

                def keys(a):
                    next_unit_ready()
                    claim(a)
                    wh, wl = (w.rearrange("p (k h n) -> p k h n", k=2, h=2) for w in unit())
                    for hh in range(2):
                        for k in range(2):
                            mm = product(bank(a, hh), (wh[:, k, hh, 0:NOPE], wl[:, k, hh, 0:NOPE]),
                                         (UHI[3 + k], ULO[3 + k]), k == 0, k == 1)
                    mm.then_inc(psum_done, 1)
                    c.add("psum_done")

                def values(a):
                    claim(a)
                    wh, wl = (w.rearrange("p (k h n) -> p k h n", k=2, h=2) for w in unit())
                    for t in range(QB):
                        at = slice(t * P, (t + 1) * P)
                        out = area(a)[:, t * 256:(t + 1) * 256].rearrange("p (h n) -> p h n", h=2)
                        for k in range(2):
                            mm = product(out, (UHI[3 + k][:, at], ULO[3 + k][:, at]),
                                         (wh[:, k, :, NOPE:], wl[:, k, :, NOPE:]), k == 0, k == 1)
                    mm.then_inc(unit_done, 1)
                    c.add("tensor_unit")

                def swap(a, source, claimed=True):
                    if not claimed:
                        claim(a)
                    c.add("rows")
                    pe.wait_ge(rows_ready, c.now("rows"))
                    swap_rows(bank(a, 1), 0, source).then_inc(psum_done, 1)
                    c.add("psum_done")

                def attention(half):
                    qn, kn, qr, kr, v = (mla_m[n] for n in ("qn", "kn", "qr", "kr", "v"))

                    def scores(i):
                        rows = slice(ROPE * (i % 2), ROPE * (i % 2) + ROPE)
                        for a, blocks in ((0, (3, 2)), (1, (1, 0))):
                            claim(a)
                            for b in blocks:
                                keys_n = P * (b + 1)
                                at = S_OFF[b] - (0 if a == 0 else 896)
                                out = area(a)[:, at:at + keys_n]
                                q_at = slice(b * P, (b + 1) * P)
                                nc.tensor.matmul(out, chunk(qn, i)[:, q_at], chunk(kn, i)[:, 0:keys_n],
                                                 start=True, stop=False)
                                mm = nc.tensor.matmul(out, chunk(qr, i // 2)[rows, q_at], kr[rows, 0:keys_n],
                                                      start=False, stop=True)
                            mm.then_inc(psum_done, 1)
                            c.add("psum_done")

                    def transposes(i):
                        c.add("p")
                        pe.wait_ge(p_ready, c.now("p"))
                        p = mla_m["p"][:, (i % 2) * ATT:(i % 2 + 1) * ATT]
                        for a, tiles in ((2, (0, 1)), (3, (2, 3))):
                            claim(a)
                            for j in tiles:
                                for b in range(j, QB):
                                    at = T_OFF[j] + P * (b - j) - (0 if a == 2 else 896)
                                    mm = nc.tensor.transpose(area(a)[:, at:at + P],
                                                             p[:, S_OFF[b] + P * j:S_OFF[b] + P * (j + 1)], ident)
                            mm.then_inc(psum_done, 1)
                            c.add("psum_done")

                    def weighted(i):
                        pe.wait_ge(area_free[2], c.at("area2"))
                        pe.wait_ge(area_free[3], c.at("area3"))
                        claim(4)
                        for jt in range(QB):
                            n = T - P * jt
                            mm = nc.tensor.matmul(bank(3, 1)[:, P * jt:T], v[:, jt * T + i * VD:jt * T + (i + 1) * VD],
                                                  mla_m["pt"][:, T_OFF[jt]:T_OFF[jt] + n],
                                                  start=jt == 0, stop=jt == QB - 1, skip_group_check=True)
                        mm.then_inc(psum_done, 1)
                        c.add("psum_done")

                    for i in range(HALF_HEADS + 2):
                        if i < HALF_HEADS:
                            scores(i)
                        if i >= 2:
                            weighted(i - 2)
                        if 1 <= i <= HALF_HEADS:
                            transposes(i - 1)

                pe.wait_ge(area_free[1], c.at("area1"))
                for half in range(2):
                    queries((0, 1))
                    if half == 0:
                        swap(2, mla_m["kr"], claimed=False)
                        claim(3)
                        pe.wait_ge(squares_added, c.now("squares_added") + 3)
                        column_sums(3, mla_m["rkv"]).then_inc(psum_done, 1)
                        c.add("psum_done")
                        c.add("squares_added", 3)
                    queries((2, 3))
                    swap(1, chunk(mla_m["qr"], 0))
                    keys(0)
                    swap(3, chunk(mla_m["qr"], 1))
                    values(1)
                    keys(2)
                    if half == 0:
                        pe.wait_ge(rstd_ready, c.now("rstd") + 3)
                        c.add("rstd", 3)
                        token_columns(3, mla_m["rkv"])
                    values(3)
                    pe.wait_ge(area_free[3], c.at("area3"))
                    attention(half)

                base = c.now("area4") - H
                for g in range(2):
                    def heads(kp):
                        pe.wait_ge(area_free[4], base + 2 * kp + 2)
                    square_group((0, 1) if g == 0 else (2, 3), OHI, OLO, heads if g == 0 else anything)

            def lru():
                square_group((0, 1), HI, LO, h_chunks, {3: norm_sums(2)})
                c.add("h", 8)
                c.add("rstd")
                square_group((2, 3), HI, LO, anything)

                def gates(half):
                    next_unit_ready()
                    wh, wl = unit()
                    for n in range(4):
                        k = 4 * half + n
                        claim(n % 2)
                        pe.wait_ge(xc_ready, k + 1)
                        for b in range(2):
                            at = slice(b * T + n * P, b * T + (n + 1) * P)
                            mm = product(bank(n % 2, b), (wh[:, at], wl[:, at]), (UHI[k], ULO[k]), True, True)
                        if n < 3:
                            mm.then_inc(psum_done, 1)
                            c.add("psum_done")
                    mm.then_inc(unit_done, 1)
                    c.add("tensor_unit")

                jobs["gates", 0], jobs["gates", 1] = c.now("area0"), c.now("area1")
                gates(0)
                square_group((2, 3), HI, LO, anything)
                jobs["gate", 0] = c.now("area2"), c.now("area3")
                gates(1)
                square_group((2, 3), HI, LO, anything)
                jobs["gate", 1] = c.now("area2"), c.now("area3")
                down(0)
                down(1)

            def swa():
                def swaps(a, p):
                    def run():
                        pe.wait_ge(biased, 2 * p + 2)
                        claim(a)
                        for b in range(2):
                            mm = swap_rows(bank(a, b), 1, chunk(swa_m["q"], 2 * p + b) if p < 4
                                           else chunk(swa_m["p"], b))
                        mm.then_inc(psum_done, 1)
                        c.add("psum_done")
                    return run

                def both(f, g):
                    def run():
                        f()
                        g()
                    return run

                square_group((0, 1), HI, LO, h_chunks, {3: norm_sums(2)})
                jobs["q", 0], jobs["q", 1] = c.now("area0"), c.now("area1")
                c.add("h", 8)
                jobs["q", 2], jobs["q", 3] = c.now("area2") + 1, c.now("area3") + 1
                square_group((2, 3), HI, LO, anything, {3: both(swaps(0, 0), swaps(1, 1))})
                claim(0)
                claim(1)
                jobs["k"] = c.now("area0")
                for kp in range(4):
                    if kp == 2:
                        pe.wait_ge(rstd_ready, c.now("rstd") + 1)
                        token_columns(2, rstd)
                        swaps(2, 2)()
                    if kp == 3:
                        swaps(3, 3)()
                    next_unit_ready()
                    wh, wl = unit()
                    for kk in range(2):
                        k = 2 * kp + kk
                        for m in range(2):
                            at = slice(kk * T + m * P, kk * T + (m + 1) * P)
                            mm = product(bank(0, m), (wh[:, at], wl[:, at]), (HI[k], LO[k]), k == 0, k == KC - 1)
                        for t in range(QB):
                            tok = slice(t * P, (t + 1) * P)
                            at = slice(kk * T + 256, kk * T + 512)
                            mm = product(area(1)[:, t * 256:(t + 1) * 256], (HI[k][:, tok], LO[k][:, tok]),
                                         (wh[:, at], wl[:, at]), k == 0 and t % 2 == 0, k == KC - 1, skip=True)
                    mm.then_inc(unit_done, 1)
                    c.add("tensor_unit")
                c.add("rstd")
                swaps(2, 4)()

                def scores(i, half):
                    claim(half)
                    for b in (2 * half, 2 * half + 1):
                        for a in range(2):
                            rows = slice(64 * a, 64 * a + 64)
                            n = 256 if b else 128
                            mm = nc.tensor.matmul(bank(half, a)[:, b % 2 * 256:b % 2 * 256 + n],
                                                  chunk(swa_m["q"], i)[rows, b * P:(b + 1) * P],
                                                  chunk(swa_m["kd"], i // 2)[rows, (b + 1) * P - n:(b + 1) * P],
                                                  start=True, stop=True, skip_group_check=True)
                    mm.then_inc(psum_done, 1)
                    c.add("psum_done")

                def transposes(i, half):
                    if half == 0:
                        c.add("p")
                        pe.wait_ge(p_ready, c.now("p"))
                    p = swa_m["p"][:, (i % 2) * W_ATT:(i % 2 + 1) * W_ATT]
                    claim(2)
                    at = 0
                    for j in (2 * half, 2 * half + 1):
                        for a in range(2):
                            for b in (j, j + 1):
                                if b < QB:
                                    off = a * P if b == 0 else 256 + (b - 1) * 512 + a * 256 + (j - b + 1) * P
                                    mm = nc.tensor.transpose(area(2)[:, at:at + P], p[:, off:off + P], ident)
                                    at += P
                    mm.then_inc(psum_done, 1)
                    c.add("psum_done")

                def weighted(i):
                    pe.wait_ge(area_free[2], c.at("area2"))
                    pe.wait_ge(area_free[3], c.at("area3"))
                    claim(4)
                    for a in range(2):
                        for j in range(QB):
                            n = 256 if j < 3 else 128
                            at = j * 512 + a * n
                            v_at = j * 256 + (i // 2) * 64
                            mm = nc.tensor.matmul(bank(3, 1)[64 * a:64 * a + 64, j * P:j * P + n],
                                                  swa_m["v"][:, v_at:v_at + 64], swa_m["pt"][:, at:at + n],
                                                  start=j == 0, stop=j == 3, skip_group_check=True)
                    mm.then_inc(psum_done, 1)
                    c.add("psum_done")

                need(pe, area_free[3], c.at("area3"))
                c.add("mixed")
                pe.wait_ge(mixed, c.now("mixed"))
                for i in range(KC + 2):
                    if i < KC:
                        scores(i, 0)
                    if i >= 2:
                        weighted(i - 2)
                    if 1 <= i <= KC:
                        transposes(i - 1, 0)
                    if i < KC:
                        scores(i, 1)
                    if 1 <= i <= KC:
                        transposes(i - 1, 1)
                base = c.now("area4") - KC
                for g in range(2):
                    def heads(kp):
                        pe.wait_ge(area_free[4], base + 2 * kp + 2)
                    square_group((0, 1) if g == 0 else (2, 3), UHI, ULO, heads if g == 0 else anything)

            pe.wait_ge(ones_set, 1)
            pe.wait_ge(const_loaded, 16)
            for kind, i in PHASES:
                if kind == "mla":
                    mla(i)
                elif kind == "mlp":
                    mlp()
                    c.add("rstd")
                elif kind == "lru":
                    lru()
                elif kind == "swa":
                    swa()
                else:
                    norm_sums(2)()
                passed.append(dict(c.n))

        @block.vector
        def _(dve):
            c = Counts()

            def link(ins):
                ins.then_inc(vec_step, 1)
                c.add("vec_step")
                dve.wait_ge(vec_step, c.now("vec_step"))

            def free(ins, a):
                ins.then_inc(area_free[a], 1)
                c.add(f"area{a}")

            def exact(t):
                return t.bitcast(F32)

            def split(n):
                for _ in range(n):
                    if c.now("unit") == len(units):
                        return
                    at = c.now("unit") % SLOTS * UNIT
                    to = slice(at, at + units[c.now("unit")][-1])
                    dve.wait_ge(w_hi_done, c.at("unit", 1))
                    nc.vector.tensor_tensor(w_lo[:, to], w_raw[:, to], exact(w_hi[:, to]), ALU.subtract
                                            ).then_inc(w_ready, 1)
                    c.add("unit")

            def sum_ready():
                c.add("psum_done")
                dve.wait_ge(psum_done, c.at("psum_done"))

            def units_passed(n):
                c.add("tensor_unit", n)
                dve.wait_ge(unit_done, c.at("tensor_unit"))

            def rstd_now():
                dve.wait_ge(rstd_ready, c.now("rstd"))

            def prepare(p, gain):
                for k in (2 * p, 2 * p + 1):
                    c.add("h")
                    c.add("squares")
                    dve.wait_ge(h_hi_done, c.now("h"))
                    nc.vector.scalar_tensor_tensor(out=LO[k], in0=chunk(x, k), scalar=col(*gain(k)),
                                                   in1=exact(HI[k]), op0=ALU.mult, op1=ALU.subtract
                                                   ).then_inc(h_ready, 1)

            def inverse_root():
                c.add("root")
                dve.wait_ge(root_done, c.now("root"))
                nc.vector.reciprocal(root[:, :], root[:, :]).then_inc(inv_done, 1)

            def norm_scale(a=2):
                sum_ready()
                c.add("root")
                dve.wait_ge(root_done, c.now("root"))
                free(nc.vector.tensor_scalar(var[:, :], bank(a), 1.0 / D, EPS, ALU.mult, ALU.add), a)
                nc.vector.reciprocal(root[:, :], root[:, :]).then_inc(inv_done, 1)
                c.add("rstd")

            def inner_norm_scale(a, n):
                sum_ready()
                rstd_now()
                free(nc.vector.scalar_tensor_tensor(out=var[:, :], in0=bank(a), scalar=1.0 / n, in1=rstd2[:, :],
                                                    op0=ALU.mult, op1=ALU.mult), a)
                dve.wait_ge(area_free[a], c.at(f"area{a}"))
                nc.vector.tensor_scalar(var[:, :], var[:, :], EPS, None, ALU.add).then_inc(var_ready, 1)
                inverse_root()
                c.add("rstd")

            def squared_relu(g):
                a = 2 * g
                for q in range(2):
                    c.add(f"area{a + q}")
                    dve.wait_ge(area_free[a + q], c.at(f"area{a + q}"))
                    r = chunk(mlp_m["relu"], 2 * q, 2)
                    nc.vector.tensor_tensor(r, r, r, ALU.mult).then_inc(squared, 1)
                for q in range(2):
                    c.add("u_hi")
                    dve.wait_ge(u_hi_done, c.at("u_hi"))
                    nc.vector.tensor_tensor(chunk(u_lo, 2 * (a + q), 2), chunk(mlp_m["relu"], 2 * q, 2),
                                            exact(chunk(u_hi, 2 * (a + q), 2)), ALU.subtract).then_inc(u_ready, 1)
                c.add("psum_done")
                c.add("tensor_unit", 4)

            def add_scaled(g):
                for q in range(2):
                    a = 2 * g + q
                    if q == 0:
                        sum_ready()
                    else:
                        units_passed(4)
                    free(nc.vector.tensor_tensor(two(chunk(mlp_m["scaled"], 2 * q, 2)), two(area(a)),
                                                 twice(rstd2[:, :]), ALU.mult), a)
                    dve.wait_ge(area_free[a], c.at(f"area{a}"))
                    nc.vector.tensor_tensor(chunk(x, 2 * a, 2), chunk(x, 2 * a, 2), chunk(mlp_m["scaled"], 2 * q, 2),
                                            ALU.add).then_inc(x_ready, 1)

            def mlp(gain):
                split(3)
                norm_scale()
                split(1)
                with dve.Fori(0, TURNS) as turn:
                    c.begin(turn)
                    squared_relu(0)
                    split(4)
                    squared_relu(1)
                    split(4)
                    dve.wait_ge(rstd_ready, c.now("rstd"))
                    add_scaled(0)
                    split(4)
                    add_scaled(1)
                    split(4)
                    c.end(TURNS)
                squared_relu(0)
                split(4)
                squared_relu(1)
                split(4)
                for g in range(2):
                    add_scaled(g)
                    if gain:
                        prepare(2 * g, gain)
                        prepare(2 * g + 1, gain)
                    split(3 if g == 0 else 1)

            def add_product(gain, bias=None):
                for g in range(2):
                    for q in range(2):
                        a = 2 * g + q
                        if q == 0:
                            sum_ready()
                        else:
                            units_passed(4)
                        if bias is None:
                            free(nc.vector.tensor_tensor(chunk(x, 2 * a, 2), chunk(x, 2 * a, 2), area(a), ALU.add), a)
                        else:
                            for b in range(2):
                                k = 2 * a + b
                                add = nc.vector.scalar_tensor_tensor(out=chunk(x, k), in0=bank(a, b),
                                                                     scalar=col(bias, k), in1=chunk(x, k),
                                                                     op0=ALU.add, op1=ALU.add)
                            free(add, a)
                    prepare(2 * g, gain)
                    prepare(2 * g + 1, gain)
                    split(3 if g == 0 else 1)

            def rotate(rows, swapped, a, scratch, wide=False, add=True):
                f = two if wide else (lambda t: t)
                tab = (lambda t: twice(t[:, :])) if wide else (lambda t: t[:, :])
                free(nc.vector.tensor_tensor(f(scratch), f(swapped), tab(sin), ALU.mult), a)
                link(nc.vector.tensor_tensor(f(rows), f(rows), tab(cos), ALU.mult))
                if add:
                    link(nc.vector.tensor_tensor(rows, rows, scratch, ALU.add))

            kraw = swa_m["p"][:, 0:PAIR]
            nmax = small[:, 0:16]
            total = small[:, 16:32]
            inverse = small[:, 32:48]
            sink_part = small[:, 48:64]
            token_scale = small[:, 64:68]

            def head_lo(o_hi, o_lo):
                c.add("psum_done")
                c.add("o_hi")
                dve.wait_ge(o_hi_done, c.now("o_hi"))
                free(nc.vector.tensor_tensor(o_lo, bank(3, 1), exact(o_hi), ALU.subtract), 4)

            def mla(j, gain):
                split(3)
                norm_scale()
                split(1)
                def lo(t, a, b):
                    g = col("q_norm", 3 * j + t) if t < 3 else col("kv_norm", 2 * j + t - 3)
                    c.add("squares")
                    dve.wait_ge(squares, c.now("squares"))
                    return nc.vector.scalar_tensor_tensor(out=ULO[t], in0=bank(a, b), scalar=g, in1=exact(UHI[t]),
                                                          op0=ALU.mult, op1=ALU.subtract)
                c.add("psum_done")
                c.add("tensor_unit", 4)
                for t in range(4):
                    ins = lo(t, t // 2, t % 2)
                    if t % 2:
                        free(ins, t // 2)
                units_passed(2)
                rstd_now()
                nc.vector.tensor_tensor(mla_m["kr"], bank(3, 1), rstd[:, :], ALU.mult).then_inc(rows_ready, 1)
                free(lo(4, 3, 0), 3)
                split(2)
                inner_norm_scale(2, QL)

                def nope_queries(n, a):
                    free(nc.vector.tensor_tensor(two(chunk(mla_m["qn"], 2 * n, 2)), two(area(a)), twice(mla_m["rq"]),
                                                 ALU.mult), a)

                def rotary_queries(n, a):
                    nc.vector.tensor_tensor(chunk(mla_m["qr"], n), bank(a), mla_m["rq"], ALU.mult
                                            ).then_inc(rows_ready, 1)

                def finish(n, a):
                    sum_ready()
                    rotate(chunk(mla_m["qr"], n), bank(a, 1), a, mla_m["rope"])

                def keys(n, a, wait=True):
                    if wait:
                        sum_ready()
                    free(nc.vector.tensor_tensor(two(chunk(mla_m["kn"], 2 * n, 2)), two(area(a)), twice(mla_m["rkv"]),
                                                 ALU.mult), a)

                def values(n, a):
                    units_passed(1)
                    out = mla_m["v"].rearrange("p (t n) -> p t n", t=QB)[:, :, n * 256:(n + 1) * 256]
                    free(nc.vector.tensor_tensor(out, area(a).rearrange("p (t n) -> p t n", t=QB),
                                                 token_scale.unsqueeze(2).to_broadcast([P, QB, 256]), ALU.mult), a)

                def attention(half):
                    for i in range(HALF_HEADS + 2):
                        at = 4 * (i % 2)
                        if i < HALF_HEADS:
                            for a, blocks in ((0, (3, 2)), (1, (1, 0))):
                                sum_ready()
                                off = 0 if a == 0 else 896
                                for b in blocks:
                                    edge = S_OFF[b] - off + P * b + CHUNK
                                    ins = nc.vector.memset(area(a)[0:CHUNK, edge:edge + CHUNK], NEG)
                                link(ins)
                                for b in blocks:
                                    s = area(a)[:, S_OFF[b] - off:S_OFF[b] - off + P * (b + 1)]
                                    ins = nc.vector.tensor_reduce(nmax[:, at + b:at + b + 1], s, AX.X, ALU.max,
                                                                  negate=True)
                                ins.then_inc(nmax_ready, 1)
                                c.add(f"area{a}")
                        if i >= 2:
                            h = half * HALF_HEADS + i - 2
                            head_lo(OHI[h], OLO[h])
                        if 1 <= i <= HALF_HEADS:
                            c.add("psum_done")
                            c.add("area2")
                            sum_ready()
                            free(nc.vector.tensor_copy(mla_m["pt"][:, 896:ATT], area(3)[:, 0:384]), 3)
                        if i < HALF_HEADS:
                            dve.wait_ge(area_free[1], c.at("area1"))
                            link(nc.vector.reciprocal(inverse[:, at:at + 4], total[:, at:at + 4]))
                            for b in range(QB):
                                p = mla_m["p"][:, (i % 2) * ATT + S_OFF[b]:(i % 2) * ATT + S_OFF[b] + P * (b + 1)]
                                ins = nc.vector.tensor_scalar(p, p, inverse[:, at + b:at + b + 1], None, ALU.mult)
                            ins.then_inc(p_ready, 1)

                for half in range(2):
                    sum_ready()
                    if half == 0:
                        sum_ready()
                        dve.wait_ge(table_done, tables["mla", j])
                        rotate(mla_m["kr"], bank(2, 1), 2, mla_m["rope"])
                        inner_norm_scale(3, KVL)
                        dve.wait_ge(rstd_ready, c.now("rstd") - 1)
                    nope_queries(0, 0)
                    units_passed(1)
                    rotary_queries(0, 1)
                    split(1)
                    sum_ready()
                    nope_queries(1, 2)
                    units_passed(1)
                    rotary_queries(1, 3)
                    split(1)
                    finish(0, 1)
                    if half == 0:
                        rstd_now()
                    keys(0, 0)
                    finish(1, 3)
                    if half == 0:
                        c.add("psum_done", 2)
                        dve.wait_ge(psum_done, c.now("psum_done"))
                        free(nc.vector.tensor_copy(token_scale, bank(3)[:, 0:4]), 3)
                        dve.wait_ge(area_free[3], c.at("area3"))
                    values(0, 1)
                    keys(1, 2, wait=half == 1)
                    values(1, 3)
                    split(2)
                    attention(half)
                split(4)
                add_product(gain)

            def softplus_of_lambda():
                e, z, z2, s, m = (small[:, 8 * n:8 * n + 8] for n in range(1, 6))
                dve.wait_ge(lam_exp, 1)
                link(nc.vector.tensor_scalar(s, e, 2.0, None, ALU.add))
                link(nc.vector.reciprocal(s, s))
                link(nc.vector.tensor_tensor(z, e, s, ALU.mult))
                link(nc.vector.tensor_tensor(z2, z, z, ALU.mult))
                link(nc.vector.tensor_scalar(s, z2, 1.0 / 17, None, ALU.mult))
                for d in (15, 13, 11, 9, 7, 5, 3):
                    link(nc.vector.scalar_tensor_tensor(out=s, in0=s, scalar=1.0 / d, in1=z2, op0=ALU.add,
                                                        op1=ALU.mult))
                link(nc.vector.scalar_tensor_tensor(out=s, in0=s, scalar=1.0, in1=z, op0=ALU.add, op1=ALU.mult))
                link(nc.vector.tensor_scalar(m, col("lambda", 0, 8), -1.0, 0.0, ALU.mult, ALU.max))
                link(nc.vector.scalar_tensor_tensor(out=s, in0=s, scalar=2.0, in1=m, op0=ALU.mult, op1=ALU.add))
                link(nc.vector.tensor_scalar(sp4, s, 4.0, None, ALU.mult))
                nc.vector.tensor_scalar(spm8, s, -8.0, None, ALU.mult).then_inc(softplus, 1)

            def lru(gain):
                m = lru_m
                xpad = [m["xpad"][:, b * (T + 3):(b + 1) * (T + 3)] for b in range(2)]
                softplus_of_lambda()
                split(3)
                norm_scale()
                split(1)
                for b in range(2):
                    link(nc.vector.memset(xpad[b][:, 0:3], 0.0))

                def conv(k):
                    a, pad, out = k // 2, xpad[k % 2], chunk(m["xc"], k)
                    ins = nc.vector.tensor_tensor(pad[:, 3:], bank(a, k % 2), rstd[:, :], ALU.mult)
                    if k % 2:
                        free(ins, a)
                        dve.wait_ge(area_free[a], c.at(f"area{a}"))
                    else:
                        link(ins)
                    link(nc.vector.tensor_scalar(out, pad[:, 0:T], col("conv_w", k), col("conv_b", k),
                                                 ALU.mult, ALU.add))
                    for w in range(1, 4):
                        ins = nc.vector.scalar_tensor_tensor(out=out, in0=pad[:, w:w + T], scalar=col("conv_w", 8 * w + k),
                                                             in1=out, op0=ALU.mult, op1=ALU.add)
                        if w < 3:
                            link(ins)
                    ins.then_inc(xc_done, 1)

                def xc_lo(k):
                    dve.wait_ge(xc_hi_done, k + 1)
                    nc.vector.tensor_tensor(ULO[k], chunk(m["xc"], k), exact(UHI[k]), ALU.subtract
                                            ).then_inc(xc_ready, 1)

                def gate_in(g):
                    for q in range(2):
                        if q == 0:
                            sum_ready()
                        else:
                            units_passed(4)
                        free(nc.vector.tensor_tensor(two(chunk(m["gate"], 4 * g + 2 * q, 2)), two(area(2 + q)),
                                                     twice(rstd[:, :]), ALU.mult), 2 + q)

                def recurrence(k):
                    b = k % 2
                    r, i, t = (m[n][:, b * T:(b + 1) * T] for n in ("r", "i", "t"))
                    xc = chunk(m["xc"], k)
                    dve.wait_ge(decay_in, k + 1)
                    link(nc.vector.tensor_tensor(i, i, xc, ALU.mult))
                    ins = nc.vector.scalar_tensor_tensor(out=r, in0=r, scalar=1.0, in1=t, op0=ALU.add, op1=ALU.mult)
                    ins.then_inc(decay_used, 1)
                    dve.wait_ge(decay_used, k + 1)
                    link(nc.vector.tensor_scalar(r, r, -1.0, 1.0, ALU.mult, ALU.add))
                    dve.wait_ge(roots, k + 1)
                    link(nc.vector.scalar_tensor_tensor(out=t, in0=r, scalar=1.0, in1=t, op0=ALU.add, op1=ALU.mult))
                    link(nc.vector.tensor_tensor(i, i, t, ALU.mult))
                    nc.vector.tensor_tensor_scan(xc, r, i, 0.0, ALU.mult, ALU.add).then_inc(scanned, 1)
                    dve.wait_ge(scanned, k + 1)

                def gates_passed():
                    c.add("psum_done", 3)
                    c.add("tensor_unit")
                    c.add("area0", 2)
                    c.add("area1", 2)

                def y(p):
                    c.add("gate")
                    dve.wait_ge(gate_done, c.now("gate"))
                    g = chunk(m["gate"], 2 * p, 2)
                    nc.vector.tensor_tensor(g, g, chunk(m["xc"], 2 * p, 2), ALU.mult).then_inc(y_done, 1)

                def y_lo(p):
                    c.add("u_hi")
                    dve.wait_ge(u_hi_done, c.now("u_hi"))
                    nc.vector.tensor_tensor(chunk(u_lo, 2 * p, 2), chunk(m["gate"], 2 * p, 2),
                                            exact(chunk(u_hi, 2 * p, 2)), ALU.subtract).then_inc(u_ready, 1)

                rstd_now()
                for g in range(2):
                    for k in range(4 * g, 4 * g + 4):
                        if k % 4 == 0:
                            sum_ready()
                        if k % 4 == 2:
                            units_passed(4)
                        conv(k)
                        if k % 4:
                            xc_lo(k - 1)
                        if k == 5:
                            split(1)
                    xc_lo(4 * g + 3)
                    if g == 0:
                        split(4)
                gates_passed()
                recurrence(0)
                recurrence(1)
                split(2)
                recurrence(2)
                recurrence(3)
                split(1)
                gate_in(0)
                split(2)
                gates_passed()
                for k in range(4, 8):
                    recurrence(k)
                y(0)
                y(1)
                y_lo(0)
                y_lo(1)
                split(4)
                gate_in(1)
                y(2)
                y(3)
                y_lo(2)
                y_lo(3)
                split(4)
                add_product(gain)

            def swa(gain):
                m = swa_m
                scratch = m["p"][:, PAIR:2 * PAIR]
                split(3)
                norm_scale()
                split(1)
                rstd_now()

                def rows_in(g):
                    for a in (2 * g, 2 * g + 1):
                        free(nc.vector.tensor_tensor(two(chunk(m["q"], 2 * a, 2)), two(area(a)), twice(rstd[:, :]),
                                                     ALU.mult), a)
                sum_ready()
                units_passed(4)
                rows_in(0)
                split(3)
                dve.wait_ge(table_done, tables["swa", 0])
                for p in range(2):
                    sum_ready()
                    rotate(chunk(m["q"], 2 * p, 2), area(p), p, scratch, wide=True)
                split(1)
                sum_ready()
                units_passed(4)
                rows_in(1)
                split(2)
                sum_ready()
                free(nc.vector.tensor_copy(token_scale, bank(2)[:, 0:4]), 2)
                sum_ready()
                rotate(chunk(m["q"], 4, 2), area(2), 2, scratch, wide=True)
                split(1)
                sum_ready()
                rotate(chunk(m["q"], 6, 2), area(3), 3, scratch, wide=True)
                split(1)
                units_passed(4)
                free(nc.vector.tensor_tensor(two(kraw), two(area(0)), twice(rstd[:, :]), ALU.mult), 0)
                dve.wait_ge(extra_loaded, 32)
                for t in range(QB):
                    ins = nc.vector.scalar_tensor_tensor(out=m["v"][:, t * 256:(t + 1) * 256],
                                                         in0=area(1)[:, t * 256:(t + 1) * 256],
                                                         scalar=token_scale[:, t:t + 1], in1=m["bv"],
                                                         op0=ALU.mult, op1=ALU.add)
                free(ins, 1)
                sum_ready()
                rotate(kraw, area(2), 2, scratch, wide=True, add=False)
                for g in range(SW_G):
                    src = slice(64 * (g % 2), 64 * (g % 2) + 64)
                    for half in range(2):
                        ins = nc.vector.tensor_tensor(chunk(m["kd"], g)[64 * half:64 * half + 64, :],
                                                      chunk(kraw, g // 2)[src, :], chunk(scratch, g // 2)[src, :],
                                                      ALU.add)
                ins.then_inc(mixed, 1)
                dve.wait_ge(mixed, 1)

                dve.wait_ge(const_loaded, 16)
                mask = const[:, C_MASK:C_MASK + 256]
                for i in range(KC + 2):
                    at = 8 * (i % 2)
                    p = m["p"][:, (i % 2) * W_ATT:(i % 2 + 1) * W_ATT]

                    def blocks(b):
                        n = 256 if b else 128
                        return n, (0 if b == 0 else 256 + (b - 1) * 512)

                    def masked(half):
                        sum_ready()
                        for b in (2 * half, 2 * half + 1):
                            n, off = blocks(b)
                            for a in range(2):
                                ins = nc.vector.tensor_tensor_reduce(
                                    out=p[:, off + a * n:off + (a + 1) * n],
                                    in0=bank(half, a)[:, b % 2 * 256:b % 2 * 256 + n],
                                    in1=mask[:, 256 - n:256], scale=SW_D ** -0.5,
                                    scalar=m["sinks"][:, 2 * i + a:2 * i + a + 1], op0=ALU.add, op1=ALU.max,
                                    accum_out=nmax[:, at + 2 * b + a:at + 2 * b + a + 1])
                        free(ins, half)

                    if i < KC:
                        masked(0)
                    if i >= 2:
                        head_lo(UHI[i - 2], ULO[i - 2])
                    if 1 <= i <= KC:
                        c.add("psum_done")
                        c.add("area2")
                    if i < KC:
                        masked(1)
                        dve.wait_ge(area_free[1], c.at("area1"))
                        nm = nmax[:, at:at + 8]
                        link(nc.vector.tensor_scalar(nm, nm, -1.0, None, ALU.mult))
                        nc.vector.tensor_tensor(sink_part[:, at:at + 8].rearrange("p (b a) -> p b a", a=2),
                                                nm.rearrange("p (b a) -> p b a", a=2),
                                                m["sinks"][:, 2 * i:2 * i + 2].unsqueeze(1).to_broadcast([P, QB, 2]),
                                                ALU.add).then_inc(nmax_ready, 1)
                    if 1 <= i <= KC:
                        sum_ready()
                        free(nc.vector.tensor_copy(m["pt"][:, PAIR:W_ATT], area(2)[:, 0:W_ATT - PAIR]), 2)
                    if i < KC:
                        c.add("exp")
                        dve.wait_ge(exp_done, c.now("exp"))
                        s8 = slice(at, at + 8)
                        link(nc.vector.tensor_tensor(total[:, s8], total[:, s8], sink_part[:, s8], ALU.add))
                        link(nc.vector.reciprocal(inverse[:, s8], total[:, s8]))
                        for b in range(QB):
                            n, off = blocks(b)
                            for a in range(2):
                                q = p[:, off + a * n:off + (a + 1) * n]
                                k = at + 2 * b + a
                                ins = nc.vector.tensor_scalar(q, q, inverse[:, k:k + 1], None, ALU.mult)
                        ins.then_inc(p_ready, 1)
                split(4)
                add_product(gain, "swa_b_o")

            def final():
                norm_scale()
                rstd_now()
                for k in range(KC):
                    nc.vector.scalar_tensor_tensor(out=chunk(arena, k), in0=chunk(x, k), scalar=col("norm_final", k),
                                                   in1=rstd[:, :], op0=ALU.mult, op1=ALU.mult).then_inc(out_ready, 1)

            dve.wait_ge(cols_loaded, 16)
            for p in range(4):
                prepare(p, gains(-1))
                split(1)
            for n, (kind, i) in enumerate(PHASES):
                if kind == "final":
                    final()
                else:
                    {"mla": lambda g: mla(i, g), "mlp": mlp, "lru": lru, "swa": swa}[kind](gains(n))
                for name in ("psum_done", "tensor_unit", "area0", "area1", "area2", "area3", "area4"):
                    assert c.now(name) == passed[n].get(name, 0), (kind, i, name, c.now(name), passed[n])

        @block.scalar
        def _(act):
            c = Counts()
            act.wait_ge(cols_loaded, 16)

            def link(ins):
                ins.then_inc(act_step, 1)
                c.add("act_step")
                act.wait_ge(act_step, c.now("act_step"))

            def split(n):
                for _ in range(n):
                    if c.now("unit") == len(units):
                        return
                    u = units[c.now("unit")]
                    slot = c.now("unit") % SLOTS
                    to = slice(slot * UNIT, slot * UNIT + u[-1])
                    c.add(f"loaded{slot}", 16 * LOADS.get(u[0], 1))
                    act.wait_ge(w_loaded[slot], c.at(f"loaded{slot}"))
                    need(act, unit_done, c.at("unit", 1 - SLOTS))
                    nc.scalar.activation(w_hi[:, to], w_raw[:, to], ACT.Copy).then_inc(w_hi_done, 1)
                    c.add("unit")

            def sum_ready():
                c.add("psum_done")
                act.wait_ge(psum_done, c.at("psum_done"))

            def units_passed(n):
                c.add("tensor_unit", n)
                act.wait_ge(unit_done, c.at("tensor_unit"))

            def prepare(p, gain, ready):
                ready(p)
                for k in (2 * p, 2 * p + 1):
                    if gain:
                        nc.scalar.activation(HI[k], chunk(x, k), ACT.Copy, scale=col(*gain(k))).then_inc(h_hi_done, 1)
                    if k == 0:
                        need(act, rstd_ready, c.now("rstd"))
                    if k >= 3:
                        act.wait_ge(squares_added, c.now("squares_added") + k - 2)
                    to = ssq[:, :] if k == 0 else chunk(sq, k % 2)
                    nc.scalar.activation(to, chunk(x, k), ACT.Square).then_inc(squares, 1)
                if p == 3:
                    c.add("squares_added", 7)

            def norm_root(a=2):
                sum_ready()
                need(act, rstd_ready, c.now("rstd"))
                nc.scalar.activation(root[:, :], bank(a), ACT.Sqrt, bias=eps_col, scale=1.0 / D).then_inc(root_done, 1)
                c.add("rstd")

            def inner_root():
                c.add("var")
                act.wait_ge(var_ready, c.now("var"))
                nc.scalar.activation(root[:, :], var[:, :], ACT.Sqrt).then_inc(root_done, 1)
                c.add("rstd")

            def squared_relu(g):
                a = 2 * g
                for q in range(2):
                    if q == 0:
                        sum_ready()
                    else:
                        units_passed(4)
                    if g == 1:
                        act.wait_ge(u_ready, c.at("u_ready", q - 1))
                    nc.scalar.activation(chunk(mlp_m["relu"], 2 * q, 2), area(a + q), ACT.Relu
                                         ).then_inc(area_free[a + q], 1)
                for q in range(2):
                    c.add("squared")
                    act.wait_ge(squared, c.at("squared"))
                    nc.scalar.activation(chunk(u_hi, 2 * (a + q), 2), chunk(mlp_m["relu"], 2 * q, 2), ACT.Copy
                                         ).then_inc(u_hi_done, 1)
                c.add("u_ready", 2)

            def down_passed():
                c.add("psum_done")
                c.add("tensor_unit", 4)
                c.add("x_ready", 2)

            def mlp(n, gain):
                split(3)
                norm_root()
                split(1)
                with act.Fori(0, TURNS) as turn:
                    c.begin(turn)
                    squared_relu(0)
                    split(4)
                    squared_relu(1)
                    split(4)
                    down_passed()
                    split(4)
                    down_passed()
                    split(4)
                    c.end(TURNS)
                squared_relu(0)
                split(4)
                squared_relu(1)
                split(4)
                if before_rotary(n):
                    rotary_tables()
                for g in range(2):
                    down_passed()

                    def ready(p):
                        act.wait_ge(x_ready, c.now("x_ready") - 1 + p % 2)
                    prepare(2 * g, gain, ready)
                    prepare(2 * g + 1, gain, ready)
                    split(3 if g == 0 else 1)

            def after_mixer(n, gain):
                def ready(p):
                    act.wait_ge(area_free[p], passed[n][f"area{p}"])
                for g in range(2):
                    c.add("psum_done")
                    c.add("tensor_unit", 4)
                    prepare(2 * g, gain, ready)
                    prepare(2 * g + 1, gain, ready)
                    split(3 if g == 0 else 1)

            def rotary_tables():
                for name, to in (("sin", sin), ("cos", cos)):
                    c.add("turns")
                    act.wait_ge(turns_ready, c.now("turns"))
                    scale = const[:, C_SIGN + rotary[(c.now("turns") - 1) // 2]:][:, 0:1] if name == "sin" else TURN
                    nc.scalar.activation(to[:, :], tab_m["sum" if name == "sin" else "rest"], ACT.Sin, scale=scale
                                         ).then_inc(table_done, 1)

            def head_hi(o_hi):
                sum_ready()
                nc.scalar.activation(o_hi, bank(3, 1), ACT.Copy).then_inc(o_hi_done, 1)

            def mla(n, j, gain):
                split(3)
                norm_root()
                split(1)
                base = c.now("squares_added")
                c.add("psum_done")
                act.wait_ge(psum_done, c.now("psum_done"))
                for t in range(5):
                    if t == 2:
                        units_passed(4)
                    if t == 4:
                        units_passed(2)
                        act.wait_ge(squares_added, base + 1)
                    source = bank(t // 2, t % 2) if t < 4 else bank(3)
                    g = col("q_norm", 3 * j + t) if t < 3 else col("kv_norm", 2 * j + t - 3)
                    nc.scalar.activation(UHI[t], source, ACT.Copy, scale=g)
                    to = (mla_m["rq"], chunk(sq, 1), chunk(sq, 0), mla_m["rkv"], chunk(sq, 1))[t]
                    nc.scalar.activation(to, source, ACT.Square).then_inc(squares, 1)
                c.add("squares_added", 3)
                if j == 0:
                    rotary_tables()
                split(2)
                c.add("psum_done")
                inner_root()
                inner_root()

                def attention(half):
                    for i in range(HALF_HEADS + 2):
                        at = 4 * (i % 2)
                        if i < HALF_HEADS:
                            for a, blocks in ((0, (3, 2)), (1, (1, 0))):
                                c.add("psum_done")
                                c.add("nmax")
                                act.wait_ge(nmax_ready, c.now("nmax"))
                                off = 0 if a == 0 else 896
                                for b in blocks:
                                    n_keys = P * (b + 1)
                                    ins = nc.scalar.activation(
                                        mla_m["p"][:, (i % 2) * ATT + S_OFF[b]:(i % 2) * ATT + S_OFF[b] + n_keys],
                                        area(a)[:, S_OFF[b] - off:S_OFF[b] - off + n_keys], ACT.Exp,
                                        bias=nmax[:, at + b:at + b + 1], accum_out=total[:, at + b:at + b + 1])
                                ins.then_inc(area_free[a], 1)
                        if i >= 2:
                            head_hi(OHI[half * HALF_HEADS + i - 2])
                        if 1 <= i <= HALF_HEADS:
                            sum_ready()
                            nc.scalar.activation(mla_m["pt"][:, 0:896], area(2)[:, 0:896], ACT.Copy
                                                 ).then_inc(area_free[2], 1)
                            c.add("psum_done")

                for half in range(2):
                    split(2)
                    split(2)
                    c.add("psum_done", 9 if half == 0 else 6)
                    c.add("tensor_unit", 4)
                    attention(half)
                split(4)
                after_mixer(n, gain)

            nmax = small[:, 0:16]
            total = small[:, 16:32]
            sink_part = small[:, 48:64]

            def lru(n, gain):
                m = lru_m
                e, s = small[:, 8:16], small[:, 0:8]
                link(nc.scalar.activation(s, col("lambda", 0, 8), ACT.Abs))
                nc.scalar.activation(e, s, ACT.Exp, scale=-1.0).then_inc(lam_exp, 1)
                split(3)
                norm_root()
                split(1)

                def xc_hi(k):
                    act.wait_ge(xc_done, k + 1)
                    nc.scalar.activation(UHI[k], chunk(m["xc"], k), ACT.Copy).then_inc(xc_hi_done, 1)

                def gates(half, batch):
                    ks = (2 * batch, 2 * batch + 1)
                    if batch:
                        act.wait_ge(scanned, 2 * batch)
                    bufs = [[m[x_][:, b * T:(b + 1) * T] for x_ in ("r", "i", "t")] for b in range(2)]
                    for k in ks:
                        if k % 4 == 3:
                            units_passed(1)
                        else:
                            sum_ready()
                        r, i, t = bufs[k % 2]
                        nc.scalar.activation(r, bank(k % 2, 0), ACT.Sigmoid, bias=col("b_rgate", k))
                        nc.scalar.activation(i, bank(k % 2, 1), ACT.Sigmoid, bias=col("b_igate", k)
                                             ).then_inc(area_free[k % 2], 1)
                        c.add(f"gates{k % 2}")
                    act.wait_ge(area_free[0], gate_jobs(0, c.now("gates0")))
                    act.wait_ge(area_free[1], gate_jobs(1, c.now("gates1")))
                    for k in ks:
                        r, i, t = bufs[k % 2]
                        nc.scalar.activation(t, r, ACT.Tanh, scale=sp4[:, k:k + 1]).then_inc(tanh_done, 1)
                    act.wait_ge(tanh_done, ks[1] + 1)
                    for k in ks:
                        r, i, t = bufs[k % 2]
                        nc.scalar.activation(r, r, ACT.Exp, scale=spm8[:, k:k + 1]).then_inc(decay_in, 1)

                def sqrt(batch):
                    for k in (2 * batch, 2 * batch + 1):
                        act.wait_ge(decay_used, k + 1)
                        t = m["t"][:, (k % 2) * T:(k % 2 + 1) * T]
                        nc.scalar.activation(t, t, ACT.Sqrt).then_inc(roots, 1)

                def gelu(g):
                    c.add("psum_done")
                    c.add("tensor_unit", 4)
                    for q in range(2):
                        act.wait_ge(area_free[2 + q], jobs["gate", g][q])
                        t = chunk(m["gate"], 4 * g + 2 * q, 2)
                        nc.scalar.activation(t, t, ACT.Gelu_apprx_tanh).then_inc(gate_done, 1)

                def y_hi(p):
                    act.wait_ge(y_done, p + 1)
                    nc.scalar.activation(chunk(u_hi, 2 * p, 2), chunk(m["gate"], 2 * p, 2), ACT.Copy
                                         ).then_inc(u_hi_done, 1)

                c.add("psum_done")
                c.add("tensor_unit", 4)
                for k in range(4):
                    xc_hi(k)
                split(4)
                c.add("psum_done")
                c.add("tensor_unit", 4)
                act.wait_ge(softplus, 1)
                gates(0, 0)
                xc_hi(4)
                xc_hi(5)
                split(1)
                xc_hi(6)
                xc_hi(7)
                sqrt(0)
                split(2)
                gates(0, 1)
                sqrt(1)
                split(1)
                gelu(0)
                split(1)
                gates(1, 2)
                split(1)
                sqrt(2)
                gates(1, 3)
                sqrt(3)
                y_hi(0)
                y_hi(1)
                split(4)
                gelu(1)
                y_hi(2)
                y_hi(3)
                c.add("u_ready", 4)
                split(4)
                after_mixer(n, gain)

            def swa(n, gain):
                m = swa_m
                split(3)
                norm_root()
                split(1)

                def bias(p, a, job):
                    act.wait_ge(area_free[a], job)
                    for k in (2 * p, 2 * p + 1):
                        t = chunk(m["q"], k) if p < 4 else chunk(m["p"], k % 2)
                        nc.scalar.activation(t, t, ACT.Identity, bias=col("swa_b_qk", k)).then_inc(biased, 1)

                c.add("psum_done", 9 - 1)
                c.add("tensor_unit", 12)
                bias(0, 0, jobs["q", 0])
                bias(1, 1, jobs["q", 1])
                split(4)
                bias(2, 2, jobs["q", 2])
                bias(3, 3, jobs["q", 3])
                split(4)
                bias(4, 0, jobs["k"])
                for i in range(KC + 2):
                    at = 8 * (i % 2)
                    if i < KC:
                        c.add("psum_done")
                    if i >= 2:
                        head_hi(UHI[i - 2])
                    if 1 <= i <= KC:
                        sum_ready()
                        nc.scalar.activation(m["pt"][:, 0:PAIR], area(2), ACT.Copy).then_inc(area_free[2], 1)
                    if i < KC:
                        c.add("psum_done")
                        c.add("nmax")
                        act.wait_ge(nmax_ready, c.now("nmax"))
                        sp = sink_part[:, at:at + 8]
                        nc.scalar.activation(sp, sp, ACT.Exp)
                        p = m["p"][:, (i % 2) * W_ATT:(i % 2 + 1) * W_ATT]
                        for b in range(QB):
                            n_keys, off = (256, 256 + (b - 1) * 512) if b else (128, 0)
                            for a in range(2):
                                q = p[:, off + a * n_keys:off + (a + 1) * n_keys]
                                k = at + 2 * b + a
                                ins = nc.scalar.activation(q, q, ACT.Exp, bias=nmax[:, k:k + 1],
                                                           accum_out=total[:, k:k + 1])
                        ins.then_inc(exp_done, 1)
                    if 1 <= i <= KC:
                        c.add("psum_done")
                split(4)
                after_mixer(n, gain)

            def gate_jobs(a, k):
                return jobs["gates", a] + k

            act.wait_ge(ones_set, 1)
            for p in range(4):
                def ready(p):
                    act.wait_ge(x_loaded[p], 16)
                prepare(p, gains(-1), ready)
                split(1)
            for n, (kind, i) in enumerate(PHASES):
                if kind == "final":
                    norm_root()
                else:
                    {"mla": lambda g: mla(n, i, g), "mlp": lambda g: mlp(n, g), "lru": lambda g: lru(n, g),
                     "swa": lambda g: swa(n, g)}[kind](gains(n))
                for name in ("psum_done", "tensor_unit"):
                    assert c.now(name) == passed[n].get(name, 0), (kind, i, name, c.now(name), passed[n])

        @block.gpsimd
        def _(pool):
            c = Counts()
            g = nc.gpsimd

            def link(ins):
                ins.then_inc(pool_step, 1)
                c.add("step")
                pool.wait_ge(pool_step, c.now("step"))

            def add_squares(to, source):
                c.add("squares")
                pool.wait_ge(squares, c.now("squares"))
                g.tensor_tensor(to, to, source, ALU.add).then_inc(squares_added, 1)
                c.add("added")
                pool.wait_ge(squares_added, c.now("added"))

            def squares_of_x():
                c.add("squares")
                for k in range(1, KC):
                    add_squares(ssq[:, :], chunk(sq, k % 2))

            def newton(t, scale=1.0):
                c.add("inv")
                pool.wait_ge(inv_done, c.now("inv"))
                link(g.tensor_tensor(t, root[:, :], root[:, :], ALU.mult))
                link(g.tensor_tensor(t, t, var[:, :], ALU.mult))
                link(g.tensor_scalar(t, t, -0.5 * scale, 1.5 * scale, ALU.mult, ALU.add))

            def norm_of_x():
                newton(ssq[:, :])
                link(g.tensor_tensor(rstd[:, :], root[:, :], ssq[:, :], ALU.mult))
                g.tensor_tensor(rstd2[:, :], rstd[:, :], rstd[:, :], ALU.mult).then_inc(rstd_ready, 1)
                c.add("rstd")
                pool.wait_ge(rstd_ready, c.now("rstd"))

            def inner_norm(name, scale):
                t = mla_m[name]
                newton(t, scale)
                link(g.tensor_tensor(t, root[:, :], t, ALU.mult))
                g.tensor_tensor(t, t, rstd[:, :], ALU.mult).then_inc(rstd_ready, 1)
                c.add("rstd")
                pool.wait_ge(rstd_ready, c.now("rstd"))

            def angles(kind):
                ang, head, rest, n, total = (tab_m[k] for k in ("ang", "head", "rest", "n", "sum"))
                parts = turn_parts()

                def times(out, in_, f):
                    link(g.tensor_scalar(out, in_, f, 0.0, ALU.mult, ALU.add))

                def whole_off(t):
                    link(g.tensor_scalar(n, t, 1.0, ROUND, ALU.mult, ALU.add))
                    link(g.tensor_scalar(n, n, 1.0, -ROUND, ALU.mult, ALU.add))
                    link(g.tensor_tensor(t, t, n, ALU.subtract))

                c.add("positions", 16)
                pool.wait_ge(pos_loaded, c.now("positions"))
                link(g.tensor_copy(ang, tab_m["pos"].bitcast(I32)))
                link(g.tensor_scalar(ang, ang, const[:, C_FREQ + kind:C_FREQ + kind + 1], 0.0, ALU.mult, ALU.add))
                times(head, ang, 4097.0)
                link(g.tensor_tensor(rest, head, ang, ALU.subtract))
                link(g.tensor_tensor(head, head, rest, ALU.subtract))
                link(g.tensor_tensor(rest, ang, head, ALU.subtract))
                times(total, head, parts[0])
                whole_off(total)
                whole_off(total)
                for source, part in ((rest, parts[0]), (head, parts[1])):
                    times(ang, source, part)
                    whole_off(ang)
                    link(g.tensor_tensor(total, total, ang, ALU.add))
                for source, part in ((rest, parts[1]), (head, parts[2]), (rest, parts[2]), (head, parts[3])):
                    times(ang, source, part)
                    link(g.tensor_tensor(total, total, ang, ALU.add))
                whole_off(total)
                link(g.tensor_scalar(rest, total, 1.0, 0.25, ALU.mult, ALU.add))
                c.add("turns")
                whole_off_last = g.tensor_scalar(n, rest, 1.0, ROUND, ALU.mult, ALU.add)
                whole_off_last.then_inc(turns_ready, 1)
                pool.wait_ge(turns_ready, c.now("turns"))
                link(g.tensor_scalar(n, n, 1.0, -ROUND, ALU.mult, ALU.add))
                g.tensor_tensor(rest, rest, n, ALU.subtract).then_inc(turns_ready, 1)
                c.add("turns")
                pool.wait_ge(turns_ready, c.now("turns"))

            g.memset(eps_col, EPS)
            g.memset(ones[:, :], 1.0).then_inc(ones_set, 1)
            squares_of_x()
            pool.wait_ge(const_loaded, 16)
            for n, (kind, i) in enumerate(PHASES):
                if kind == "mla":
                    if i == 0:
                        angles(0)
                    norm_of_x()
                    c.add("squares")
                    add_squares(mla_m["rq"], chunk(sq, 1))
                    add_squares(mla_m["rq"], chunk(sq, 0))
                    c.add("squares")
                    add_squares(mla_m["rkv"], chunk(sq, 1))
                    inner_norm("rq", SCALE)
                    inner_norm("rkv", 1.0)
                else:
                    norm_of_x()
                if kind == "mlp" and before_rotary(n):
                    angles(1 if PHASES[n + 1][0] == "swa" else 0)
                if kind != "final":
                    squares_of_x()


_OUT = (1, T, D)


def kernel(**inputs):
    import numpy as _np
    import concourse.bacc as _bacc
    from concourse import mybir as _mybir
    from concourse.bass_utils import run_bass_kernel_spmd as _run

    a = {k: _np.ascontiguousarray(v) for k, v in inputs.items()}

    def by_feature(v):
        return v.reshape(-1, P).T

    cols = _np.concatenate([by_feature(v) for v in (
        a["norm_mix"], a["norm_mlp"], a["norm_final"], a["mla_q_norm"], a["mla_kv_norm"], a["lru_conv_w"],
        a["lru_conv_b"], a["lru_b_rgate"], a["lru_b_igate"], a["lru_lambda"], a["swa_b_in"][:, :1280],
        a["swa_b_o"])], axis=1)
    arrays = {
        "x": a["x"][0].T,
        "positions": a["positions"],
        "cols": cols,
        "const": rope_constants(),
        "swa_bv": a["swa_b_in"][:, 1280:],
        "swa_sinks": a["swa_sinks"],
    }
    for name in ("mla_w_in", "mla_w_uq", "mla_w_ukv", "mla_w_o", "lru_w_in", "lru_w_rgate", "lru_w_igate",
                 "lru_w_out", "swa_w_in", "swa_w_o", "mlp_w1", "mlp_w2"):
        arrays[name] = a[name]
    arrays = {f"in_{k}": _np.ascontiguousarray(v) for k, v in arrays.items()}

    nc = _bacc.Bacc("TRN2", target_bir_lowering=False, num_devices=1)
    A = {k[3:]: nc.dram_tensor(k, v.shape, _mybir.dt.from_np(v.dtype), kind="ExternalInput").ap()
         for k, v in arrays.items()}
    A["out"] = nc.dram_tensor("out", (D, T), _mybir.dt.float32, kind="ExternalOutput").ap()
    trunk(nc, A)
    r = _run(nc, [arrays], core_ids=[0])
    got = r.results[0]["out"]
    return _np.ascontiguousarray(got.T).reshape(_OUT)
```

```python
from contextlib import ExitStack

import numpy as np

import concourse.bass as bass
from concourse import mybir

ALU = mybir.AluOpType
ACT = mybir.ActivationFunctionType
AX = mybir.AxisListType
F32 = mybir.dt.float32
F32R = mybir.dt.float32r
I32 = mybir.dt.int32

P = 128
D = 1024
T = 512
KC = D // P
F = 4 * D
DEPTH = 4
EPS = 1e-6
NEG = -1e30
CHUNK = 64
TURN = 6.283185
ROUND = 1.5 * 2.0 ** 23

H = 8
NOPE = 128
ROPE = 64
VD = 128
QL = 384
KVL = 256
SCALE = (NOPE + ROPE) ** -0.5
HALF_HEADS = H // 2
QB = T // P

SW_H = 16
SW_G = 4
SW_D = 64

SLOTS = 4
UNIT = 3 * 2 * (NOPE + ROPE)
PAIR = 2 * T
SLICE = 1024
SLICES = F // SLICE
SLICE_UNITS = 16
ARENA = 12816

S_OFF = {3: 0, 2: 512, 1: 896, 0: 1152}
T_OFF = {0: 0, 1: 512, 2: 896, 3: 1152}
ATT = 1280
W_ATT = 1792

COLS = {}
_at = 0
for _name, _n in (("norm_mix", DEPTH * 8), ("norm_mlp", DEPTH * 8), ("norm_final", 8),
                  ("q_norm", 2 * 3), ("kv_norm", 2 * 2), ("conv_w", 4 * 8), ("conv_b", 8),
                  ("b_rgate", 8), ("b_igate", 8), ("lambda", 8), ("swa_b_qk", 10), ("swa_b_o", 8)):
    COLS[_name] = _at
    _at += _n
NCOLS = _at

C_IDENT, C_PERM = 0, 128
C_MASK = C_PERM + 2 * 128
C_FREQ = C_MASK + 256
C_SIGN = C_FREQ + 2
C_BLOCK = C_SIGN + 2
C_PICK = C_BLOCK + QB
NCONST = C_PICK + 2 * 128


def rope_constants():
    c = np.zeros((P, NCONST), np.float32)
    c[:, C_IDENT:C_IDENT + P] = np.eye(P)
    for n, (rows, rot) in enumerate(((ROPE, ROPE), (SW_D, SW_D // 4))):
        half = rot // 2
        e = (-np.arange(half, dtype=np.float32) / np.float32(half)).astype(np.float64)
        freq = np.power(500000.0, e).astype(np.float32)
        for p in range(P):
            r = p % rows
            if r < rot:
                other = p + half if r < half else p - half
                c[other, C_PERM + n * P + p] = 1.0
                c[p, C_SIGN + n] = -TURN if r < half else TURN
            if p % 32 < half:
                c[p, C_FREQ + n] = freq[p % 32]
            c[(r % half if r < rot else 31)::32, C_PICK + n * P + p] = 1.0
    for b in range(QB):
        c[32 * b:32 * b + 32, C_BLOCK + b] = 1.0
    c[:CHUNK, C_MASK:C_MASK + CHUNK] = NEG
    c[:CHUNK, C_MASK + 3 * CHUNK:C_MASK + 4 * CHUNK] = NEG
    c[CHUNK:, C_MASK:C_MASK + 2 * CHUNK] = NEG
    return c


def turn_parts():
    pi = 31415926535897932384626433832795028841971693993751
    left = (10 ** 49 << 199) // pi
    parts = []
    for bits in (14, 26, 38, 50):
        unit = 1 << (200 - bits)
        part = (left + unit // 2) // unit
        parts.append(part / (1 << bits))
        left -= part * unit
    return parts


def weight_units():
    u = []

    def mlp(i):
        for s in range(SLICES):
            for g in range(2):
                u.extend(("w1", i, s, g, kp, PAIR) for kp in range(4))
            for g in range(2):
                u.extend(("w2", i, s, g, kp, PAIR) for kp in range(4))

    def square(name, j, groups, first=0):
        for g in range(groups):
            u.extend((name, j, first + g, kp, PAIR) for kp in range(4))

    def mla(j):
        square("mla_in", j, 1)
        u.extend(("mla_in_tail", j, kq, 4 * 256) for kq in range(2))
        for half in range(2):
            u.extend(("mla_uq", j, 2 * half + n, UNIT) for n in range(2))
            u.extend(("mla_ukv", j, 2 * half + n, PAIR) for n in range(2))
        square("mla_o", j, 2)

    def lru():
        square("lru_in", 0, 2, 2)
        u.append(("lru_gates", 0, PAIR))
        square("lru_in", 0, 1, 0)
        u.append(("lru_gates", 1, PAIR))
        square("lru_in", 0, 1, 1)
        square("lru_out", 0, 2)

    def swa():
        square("swa_in", 0, 1, 2)
        square("swa_in", 0, 2)
        square("swa_o", 0, 2)

    for kind, i in PHASES:
        {"mla": lambda: mla(i), "lru": lru, "swa": swa, "mlp": lambda: mlp(i), "final": lambda: None}[kind]()
    return u


LOADS = {"lru_gates": 2, "mla_in_tail": 2, "mla_uq": 4}


PHASE_UNITS = {"mla": 22, "lru": 26, "swa": 20, "mlp": SLICES * SLICE_UNITS, "final": 0}
PHASES = [("mla", 0), ("mlp", 0), ("lru", 0), ("mlp", 1), ("swa", 0), ("mlp", 2), ("mla", 1), ("mlp", 3),
          ("final", 0)]

PER_TURN = {"unit": SLICE_UNITS, "tensor_unit": SLICE_UNITS, "psum_done": 4, "squared": 4, "u_hi": 4, "u_ready": 4,
            "x_ready": 4}
PER_TURN |= {f"area{a}": 2 for a in range(4)} | {f"loaded{s}": 16 * SLICE_UNITS // SLOTS for s in range(SLOTS)}


class Counts:

    def __init__(self):
        self.n = {}
        self.turn = None

    def at(self, name, more=0):
        v = self.n.get(name, 0) + more
        assert self.turn is None or v > 0, (name, v)
        return v if self.turn is None else self.turn * PER_TURN[name] + v

    def add(self, name, k=1):
        self.n[name] = self.n.get(name, 0) + k

    def now(self, name):
        return self.n.get(name, 0)

    def begin(self, turn):
        self.turn, self.before = turn, dict(self.n)

    def end(self, turns):
        for name, v in self.n.items():
            rose = v - self.before.get(name, 0)
            assert rose in (0, PER_TURN.get(name, 0)), (name, rose)
            self.n[name] = v + rose * (turns - 1)
        self.turn = None


def need(eng, sem, value):
    if not isinstance(value, int) or value > 0:
        eng.wait_ge(sem, value)


def trunk(nc, A):
    units = weight_units()
    starts = [sum(PHASE_UNITS[k] for k, _ in PHASES[:n]) for n in range(len(PHASES))]
    assert len(units) == sum(PHASE_UNITS[k] for k, _ in PHASES)
    with ExitStack() as ctx:
        def sb(name, shape, dt=F32):
            return ctx.enter_context(nc.sbuf_tensor(name, shape, dt))

        def sem(name):
            return ctx.enter_context(nc.semaphore(name))

        psum = ctx.enter_context(nc.psum_tensor("psum", [P, 4 * PAIR], F32))

        x = sb("x", [P, KC * T])
        h_hi, h_lo = sb("h_hi", [P, KC * T], F32R), sb("h_lo", [P, KC * T], F32R)
        u_hi, u_lo = sb("u_hi", [P, KC * T], F32R), sb("u_lo", [P, KC * T], F32R)
        w_raw = sb("w_raw", [P, SLOTS * UNIT])
        w_hi, w_lo = sb("w_hi", [P, SLOTS * UNIT], F32R), sb("w_lo", [P, SLOTS * UNIT], F32R)
        ssq = sb("ssq", [P, T])
        sq = sb("sq", [P, 2 * T])
        var = sb("var", [P, T])
        root = sb("root", [P, T])
        rstd, rstd2 = sb("rstd", [P, T]), sb("rstd2", [P, T])
        cos, sin = sb("cos", [P, T]), sb("sin", [P, T])
        const = sb("const_sb", [P, NCONST])
        ones = sb("ones", [P, P])
        cols = sb("cols_sb", [P, NCOLS])
        small = sb("small", [P, 120])
        arena = sb("arena", [P, ARENA])

        def cut(*sizes):
            out, at = {}, 0
            for name, n in sizes:
                out[name] = arena[:, at:at + n]
                at += n
            assert at <= ARENA, at
            return out

        mlp_m = cut(("relu", 2 * PAIR), ("scaled", 2 * PAIR))
        mla_m = cut(("qn", 4 * T), ("qr", 2 * T), ("kn", 4 * T), ("kr", T), ("v", 4 * T), ("rq", T), ("rkv", T),
                    ("pt", ATT), ("p", 2 * ATT))
        lru_m = cut(("xc", 8 * T), ("rit01", 6 * T), ("rit23", 6 * T), ("gate0", 4 * T + 16))
        rit = [[lru_m["rit01" if n < 2 else "rit23"][:, (3 * (n % 2) + w) * T:(3 * (n % 2) + w + 1) * T]
                for w in range(3)] for n in range(4)]
        pads = [lru_m["gate0"][:, n * (T + 3):(n + 1) * (T + 3)] for n in range(4)]
        gate = [lru_m["gate0"][:, 0:PAIR], lru_m["gate0"][:, PAIR:2 * PAIR],
                lru_m["rit01"][:, 0:PAIR], lru_m["rit01"][:, PAIR:2 * PAIR]]
        swa_m = cut(("q", 8 * T), ("kd", 4 * T), ("v", 4 * 256), ("bv", 256), ("sinks", 16), ("pt", W_ATT),
                    ("p", 2 * W_ATT))
        tab_m = cut(("before", 17 * T), ("pos", P), ("ang", P), ("head", P), ("rest", P), ("n", P), ("sum", P),
                    ("wide_sin", T), ("wide_cos", T))

        eps_col = small[:, 96:97]
        sp4, spm8 = small[:, 72:80], small[:, 80:88]
        var4, root4, rstd4, step4, token_scale = (small[:, 97 + 4 * n:101 + 4 * n] for n in range(5))
        rstd2_4 = small[:, 64:68]
        diag = var

        late_squares = [arena[:, (KC + n) * T:(KC + n + 1) * T] for n in range(4)]

        ident = const[:, C_IDENT:C_IDENT + P]

        def col(name, k=0, n=1):
            return cols[:, COLS[name] + k:COLS[name] + k + n]

        def chunk(t, k, n=1):
            return t[:, k * T:(k + n) * T]

        def area(a):
            return psum[:, a * PAIR:(a + 1) * PAIR]

        def bank(a, b=0):
            return psum[:, a * PAIR + b * T:a * PAIR + (b + 1) * T]

        def twice(t):
            return t.unsqueeze(1).to_broadcast([P, 2, T])

        def two(t):
            return t.rearrange("p (a n) -> p a n", a=2)

        x_loaded = [sem(f"x_loaded{i}") for i in range(4)]
        cols_loaded = sem("cols_loaded")
        freq_loaded = sem("freq_loaded")
        const_loaded = sem("const_loaded")
        pos_loaded = sem("pos_loaded")
        extra_loaded = sem("extra_loaded")
        w_loaded = [sem(f"w_loaded{i}") for i in range(SLOTS)]
        w_hi_done = sem("w_hi_done")
        w_ready = sem("w_ready")
        unit_done = sem("unit_done")
        psum_done = sem("psum_done")
        area_free = [sem(f"area_free{a}") for a in range(5)]
        ones_set = sem("ones_set")
        h_hi_done = sem("h_hi_done")
        h_ready = sem("h_ready")
        squares = sem("squares")
        squares_added = sem("squares_added")
        var_ready = sem("var_ready")
        root_done = sem("root_done")
        diag_ready = sem("diag_ready")
        pool_step = sem("pool_step")
        squared = sem("squared")
        u_hi_done = sem("u_hi_done")
        u_ready = sem("u_ready")
        x_ready = sem("x_ready")
        vec_step = sem("vec_step")
        act_step = sem("act_step")
        turns_ready = sem("turns_ready")
        rows_ready = sem("rows_ready")
        mixed = sem("mixed")
        nmax_ready = sem("nmax_ready")
        exp_done = sem("exp_done")
        p_ready = sem("p_ready")
        o_hi_done = sem("o_hi_done")
        y_done = sem("y_done")
        gate_done = sem("gate_done")
        lam_exp = sem("lam_exp")
        softplus = sem("softplus")
        tap_done = sem("tap_done")
        xc_done = sem("xc_done")
        xc_hi_done = sem("xc_hi_done")
        xc_ready = sem("xc_ready")
        tanh_done = sem("tanh_done")
        decay_in = sem("decay_in")
        decay_used = sem("decay_used")
        roots = sem("roots")
        gated = sem("gated")
        scanned = sem("scanned")
        biased = sem("biased")
        out_ready = sem("out_ready")
        stored = sem("stored")

        HI = [chunk(h_hi, k) for k in range(KC)]
        LO = [chunk(h_lo, k) for k in range(KC)]
        UHI = [chunk(u_hi, k) for k in range(KC)]
        ULO = [chunk(u_lo, k) for k in range(KC)]
        OHI, OLO = HI[4:] + UHI[4:], LO[4:] + ULO[4:]

        def gains(n):
            if n + 1 < len(PHASES) - 1:
                layer, is_mlp = divmod(n + 1, 2)
                return lambda k: ("norm_mlp" if is_mlp else "norm_mix", 8 * layer + k)

        def before_rotary(n):
            return n + 1 < len(PHASES) and PHASES[n + 1][0] in ("swa", "mla")

        block = ctx.enter_context(nc.Block())
        TURNS = SLICES - 1
        passed = []
        jobs = {}

        def load_positions(engine):
            for t in range(QB):
                engine.dma_start(tab_m["pos"][32 * t:32 * t + 32, :].bitcast(I32),
                             A["positions"][0, t * P:(t + 1) * P].partition_broadcast(32)).then_inc(pos_loaded, 16)

        @block.sync
        def _(sp):
            c = Counts()

            def source(u, turn):
                kind = u[0]
                rows = "(a p) n -> p a n"
                if kind == "w1":
                    _, i, s, g, kp, _ = u
                    at = s * SLICE + g * T if turn is None else turn * SLICE + (s * SLICE + g * T)
                    return A["mlp_w1"][i, kp * 256:(kp + 1) * 256, bass.ds(at, T)].rearrange(rows, p=P)
                if kind == "w2":
                    _, i, s, g, kp, _ = u
                    at = s * SLICE + kp * 256 if turn is None else turn * SLICE + (s * SLICE + kp * 256)
                    return A["mlp_w2"][i, bass.ds(at, 256), g * T:(g + 1) * T].rearrange(rows, p=P)
                if kind == "mla_ukv":
                    return A["mla_w_ukv"][u[1], :, u[2] * 512:(u[2] + 1) * 512].rearrange(rows, p=P)
                name = {"mla_in": "mla_w_in", "mla_o": "mla_w_o", "lru_in": "lru_w_in", "lru_out": "lru_w_out",
                        "swa_in": "swa_w_in", "swa_o": "swa_w_o"}[kind]
                _, j, g, kp, _ = u
                return A[name][j, kp * 256:(kp + 1) * 256, g * T:(g + 1) * T].rearrange(rows, p=P)

            def load(u, turn=None):
                slot = c.now("unit") % SLOTS
                need(sp, w_ready, c.at("unit", 1 - SLOTS))
                to = w_raw[:, slot * UNIT:slot * UNIT + u[-1]]
                if u[0] == "lru_gates":
                    for n, name in enumerate(("lru_w_rgate", "lru_w_igate")):
                        sp.dma_start(to[:, n * T:(n + 1) * T].rearrange("p (b n) -> p b n", b=4),
                                     A[name][0, 4 * u[1]:4 * u[1] + 4].rearrange("b p n -> p b n")
                                     ).then_inc(w_loaded[slot], 16)
                elif u[0] == "mla_in_tail":
                    src = A["mla_w_in"][u[1], u[2] * 512:(u[2] + 1) * 512, T:T + 192].rearrange(
                        "(a p) n -> p a n", p=P)
                    to = to.rearrange("p (a n) -> p a n", a=4)
                    sp.dma_start(to[:, :, 0:192], src).then_inc(w_loaded[slot], 16)
                    sp.dma_start(to[:, :, 192:256], src[:, :, 128:192]).then_inc(w_loaded[slot], 16)
                elif u[0] == "mla_uq":
                    to = to.rearrange("p (a n) -> p a n", a=3)
                    for hh in range(2):
                        first = (2 * u[2] + hh) * (NOPE + ROPE)
                        src = A["mla_w_uq"][u[1], :, first:first + NOPE + ROPE].rearrange("(a p) n -> p a n", p=P)
                        sp.dma_start(to[:, :, hh * NOPE:(hh + 1) * NOPE], src[:, :, 0:NOPE]
                                     ).then_inc(w_loaded[slot], 16)
                        at = 2 * NOPE + hh * ROPE
                        sp.dma_start(to[:, :, at:at + ROPE], src[:, :, NOPE:]).then_inc(w_loaded[slot], 16)
                else:
                    src = source(u, turn)
                    sp.dma_start(to.rearrange("p (a n) -> p a n", n=src.shape[2]), src).then_inc(w_loaded[slot], 16)
                c.add("unit")

            sp.dma_start(cols[:, :], A["cols"]).then_inc(cols_loaded, 16)
            for p in range(4):
                sp.dma_start(two(chunk(x, 2 * p, 2)), A["x"][p * 256:(p + 1) * 256, :].rearrange(
                    "(a p) n -> p a n", p=P)).then_inc(x_loaded[p], 16)
                load(units[p])
                if p == 1:
                    for part in (slice(0, C_FREQ), slice(C_PICK, NCONST)):
                        sp.dma_start(const[:, part], A["const"][:, part]).then_inc(const_loaded, 16)
            for n, (kind, i) in enumerate(PHASES):
                start = starts[n]
                if kind == "swa":
                    sp.dma_start(swa_m["bv"], A["swa_bv"].partition_broadcast(P)).then_inc(extra_loaded, 16)
                    sp.dma_start(swa_m["sinks"], A["swa_sinks"].partition_broadcast(P)).then_inc(extra_loaded, 16)
                if kind == "mlp":
                    for u in units[max(start, c.now("unit")):start + 8]:
                        load(u)
                    with sp.Fori(0, TURNS) as turn:
                        c.begin(turn)
                        for u in units[start + 8:start + 8 + SLICE_UNITS]:
                            load(u, turn)
                        c.end(TURNS)
                    if before_rotary(n):
                        load_positions(sp)
                    for u in units[start + 56:start + 64]:
                        load(u)
                else:
                    for u in units[max(start, c.now("unit")):start + PHASE_UNITS[kind]]:
                        load(u)
            for p in range(KC // 2):
                sp.wait_ge(out_ready, p + 1)
                sp.dma_start(A["out"][p * 256:(p + 1) * 256, :].rearrange("(a p) n -> p a n", p=P),
                             two(arena[:, p * PAIR:(p + 1) * PAIR])).then_inc(stored, 16)
            sp.wait_ge(stored, 16 * (KC // 2))

        @block.tensor
        def _(pe):
            c = Counts()

            def claim(a):
                need(pe, area_free[a], c.at(f"area{a}"))
                c.add(f"area{a}")

            def unit(at=0, n=PAIR):
                slot = (c.now("tensor_unit") + at) % SLOTS
                return w_hi[:, slot * UNIT:slot * UNIT + n], w_lo[:, slot * UNIT:slot * UNIT + n]

            def next_unit_ready(at=0):
                pe.wait_ge(w_ready, c.at("tensor_unit", at + 1))

            def product(out, stat, mov, start, stop, skip=False):
                nc.tensor.matmul(out, stat[0], mov[0], start=start, stop=False, skip_group_check=skip)
                nc.tensor.matmul(out, stat[0], mov[1], start=False, stop=False, skip_group_check=skip)
                return nc.tensor.matmul(out, stat[1], mov[0], start=False, stop=stop, skip_group_check=skip)

            def column_sums(a, source, b=0):
                return nc.tensor.matmul(bank(a, b), ones[:, :], source, start=True, stop=True)

            def square_group(areas, hi, lo, ready, before_unit=None):
                claim(areas[0])
                outs = [bank(areas[0], 0), bank(areas[0], 1), bank(areas[1], 0), bank(areas[1], 1)]
                for kp in range(4):
                    if before_unit and kp in before_unit:
                        before_unit[kp]()
                    next_unit_ready()
                    ready(kp)
                    wh, wl = unit()

                    def tile(kk, m):
                        at = slice(kk * T + m * P, kk * T + (m + 1) * P)
                        k = 2 * kp + kk
                        return product(outs[m], (wh[:, at], wl[:, at]), (hi[k], lo[k]), k == 0, k == KC - 1)

                    if kp in (1, 2):
                        order = [(kk, m) for kk in range(2) for m in range(4)]
                    else:
                        order = [(kk, m) for half in range(2) for kk in range(2) for m in (2 * half, 2 * half + 1)]
                    for n, (kk, m) in enumerate(order):
                        if kp == 0 and n == 4:
                            claim(areas[1])
                        mm = tile(kk, m)
                        if kp == 3 and n == 3:
                            mm.then_inc(psum_done, 1)
                            c.add("psum_done")
                    mm.then_inc(unit_done, 1)
                    c.add("tensor_unit")

            def h_chunks(kp):
                pe.wait_ge(h_ready, c.now("h") + 2 * kp + 2)

            def anything(kp):
                pass

            def norm_sums(a):
                def run():
                    claim(a)
                    pe.wait_ge(squares_added, c.now("squares_added") + 7)
                    column_sums(a, ssq[:, :]).then_inc(psum_done, 1)
                    c.add("psum_done")
                    c.add("squares_added", 7)
                return run

            def token_sums(a, source, n):
                def run():
                    claim(a)
                    c.add("squares_added", n)
                    pe.wait_ge(squares_added, c.now("squares_added"))
                    for t in range(QB):
                        mm = nc.tensor.matmul(bank(a)[:, t:t + 1], source[:, t * P:(t + 1) * P], ones[:, 0:1],
                                              start=True, stop=True)
                    mm.then_inc(psum_done, 1)
                    c.add("psum_done")
                return run

            def spread(a, claimed=False):
                if not claimed:
                    claim(a)
                c.add("diag")
                pe.wait_ge(diag_ready, c.now("diag"))
                nc.tensor.matmul(bank(a), ones[:, :], diag[:, :], start=True, stop=True).then_inc(psum_done, 1)
                c.add("psum_done")

            def rotary_angles(which):
                def run():
                    claim(3)
                    c.add("turns", 2)
                    pe.wait_ge(const_loaded, 32)
                    pe.wait_ge(turns_ready, c.now("turns"))
                    pick = const[:, C_PICK + which * P:C_PICK + (which + 1) * P]
                    nc.tensor.matmul(bank(3, 0), pick, tab_m["wide_sin"], start=True, stop=True)
                    nc.tensor.matmul(bank(3, 1), pick, tab_m["wide_cos"], start=True, stop=True
                                     ).then_inc(psum_done, 1)
                    c.add("psum_done")
                return run

            def up(g, before_unit=None, h_wait=anything):
                square_group((0, 1) if g == 0 else (2, 3), HI, LO, h_wait, before_unit)

            def down(g):
                def ready(kp):
                    pe.wait_ge(u_ready, c.at("u_ready", kp + 1))
                square_group((0, 1) if g == 0 else (2, 3), UHI, ULO, ready if g == 0 else anything)
                if g == 1:
                    c.add("u_ready", 4)

            def mlp():
                up(0, {3: norm_sums(2)}, h_chunks)
                c.add("h", 8)
                with pe.Fori(0, TURNS) as turn:
                    c.begin(turn)
                    up(1)
                    down(0)
                    down(1)
                    up(0)
                    c.end(TURNS)
                up(1)
                down(0)
                down(1)

            def swap_rows(out, which, source):
                perm = const[:, C_PERM + which * P:C_PERM + (which + 1) * P]
                return nc.tensor.matmul(out, perm, source, start=True, stop=True)

            def mla(j):
                square_group((0, 1), HI, LO, h_chunks, {2: rotary_angles(0), 3: token_sums(2, ssq, 7)})
                c.add("h", 8)
                spread(2)
                claim(3)
                for kq in range(2):
                    if kq == 1:
                        token_sums(2, mla_m["rq"], 2)()
                    next_unit_ready()
                    wh, wl = (w.rearrange("p (a n) -> p a n", n=256) for w in unit())
                    for kk in range(4):
                        k = 4 * kq + kk
                        for b in range(2):
                            st = (wh[:, kk, b * P:(b + 1) * P], wl[:, kk, b * P:(b + 1) * P])
                            mm = product(bank(3, b), st, (HI[k], LO[k]), k == 0, k == KC - 1)
                    mm.then_inc(unit_done, 1)
                    c.add("tensor_unit")
                spread(2)

                def queries(areas):
                    next_unit_ready()
                    wh, wl = (w.rearrange("p (k n) -> p k n", k=3) for w in unit(0, UNIT))
                    claim(areas[0])
                    for hh in range(2):
                        for k in range(3):
                            at = slice(hh * NOPE, (hh + 1) * NOPE)
                            mm = product(bank(areas[0], hh), (wh[:, k, at], wl[:, k, at]),
                                         (UHI[k], ULO[k]), k == 0, k == 2)
                    mm.then_inc(psum_done, 1)
                    c.add("psum_done")
                    claim(areas[1])
                    for k in range(3):
                        mm = product(bank(areas[1]), (wh[:, k, 2 * NOPE:], wl[:, k, 2 * NOPE:]),
                                     (UHI[k], ULO[k]), k == 0, k == 2)
                    mm.then_inc(unit_done, 1)
                    c.add("tensor_unit")

                def keys(a):
                    next_unit_ready()
                    claim(a)
                    wh, wl = (w.rearrange("p (k h n) -> p k h n", k=2, h=2) for w in unit())
                    for hh in range(2):
                        for k in range(2):
                            mm = product(bank(a, hh), (wh[:, k, hh, 0:NOPE], wl[:, k, hh, 0:NOPE]),
                                         (UHI[3 + k], ULO[3 + k]), k == 0, k == 1)
                    mm.then_inc(psum_done, 1)
                    c.add("psum_done")

                def values(a):
                    claim(a)
                    wh, wl = (w.rearrange("p (k h n) -> p k h n", k=2, h=2) for w in unit())
                    for t in range(QB):
                        at = slice(t * P, (t + 1) * P)
                        out = area(a)[:, t * 256:(t + 1) * 256].rearrange("p (h n) -> p h n", h=2)
                        for k in range(2):
                            mm = product(out, (UHI[3 + k][:, at], ULO[3 + k][:, at]),
                                         (wh[:, k, :, NOPE:], wl[:, k, :, NOPE:]), k == 0, k == 1)
                    mm.then_inc(unit_done, 1)
                    c.add("tensor_unit")

                def swap(a, source, claimed=True):
                    if not claimed:
                        claim(a)
                    c.add("rows")
                    pe.wait_ge(rows_ready, c.now("rows"))
                    swap_rows(bank(a, 1), 0, source).then_inc(psum_done, 1)
                    c.add("psum_done")

                qn, kn, qr, kr, v = (mla_m[n] for n in ("qn", "kn", "qr", "kr", "v"))

                def scores(i):
                    rows = slice(ROPE * (i % 2), ROPE * (i % 2) + ROPE)
                    for a, blocks in ((0, (3, 2)), (1, (1, 0))):
                        claim(a)
                        for b in blocks:
                            keys_n = P * (b + 1)
                            at = S_OFF[b] - (0 if a == 0 else 896)
                            out = area(a)[:, at:at + keys_n]
                            q_at = slice(b * P, (b + 1) * P)
                            nc.tensor.matmul(out, chunk(qn, i)[:, q_at], chunk(kn, i)[:, 0:keys_n],
                                             start=True, stop=False)
                            mm = nc.tensor.matmul(out, chunk(qr, i // 2)[rows, q_at], kr[rows, 0:keys_n],
                                                  start=False, stop=True)
                        mm.then_inc(psum_done, 1)
                        c.add("psum_done")

                def transposes(i):
                    c.add("p")
                    pe.wait_ge(p_ready, c.now("p"))
                    p = mla_m["p"][:, (i % 2) * ATT:(i % 2 + 1) * ATT]
                    for a, tiles in ((2, (0, 1)), (3, (2, 3))):
                        claim(a)
                        for j in tiles:
                            for b in range(j, QB):
                                at = T_OFF[j] + P * (b - j) - (0 if a == 2 else 896)
                                mm = nc.tensor.transpose(area(a)[:, at:at + P],
                                                         p[:, S_OFF[b] + P * j:S_OFF[b] + P * (j + 1)], ident)
                        mm.then_inc(psum_done, 1)
                        c.add("psum_done")

                def weighted(i):
                    pe.wait_ge(area_free[2], c.at("area2"))
                    pe.wait_ge(area_free[3], c.at("area3"))
                    claim(4)
                    for jt in range(QB):
                        n = T - P * jt
                        mm = nc.tensor.matmul(bank(3, 1)[:, P * jt:T], v[:, jt * T + i * VD:jt * T + (i + 1) * VD],
                                              mla_m["pt"][:, T_OFF[jt]:T_OFF[jt] + n],
                                              start=jt == 0, stop=jt == QB - 1, skip_group_check=True)
                    mm.then_inc(psum_done, 1)
                    c.add("psum_done")

                def attention(half):
                    for i in range(HALF_HEADS + 1):
                        if i < HALF_HEADS:
                            scores(i)
                        if i >= 2:
                            weighted(i - 2)
                        if i >= 1 and (half, i) != (1, HALF_HEADS):
                            transposes(i - 1)

                pe.wait_ge(area_free[1], c.at("area1"))
                for half in range(2):
                    queries((0, 1))
                    if half == 1:
                        weighted(HALF_HEADS - 1)
                    if half == 0:
                        swap(2, mla_m["kr"], claimed=False)
                        token_sums(3, mla_m["rkv"], 1)()
                    queries((2, 3))
                    swap(1, chunk(mla_m["qr"], 0))
                    if half == 0:
                        spread(1, claimed=True)
                    keys(0)
                    if half == 1:
                        pe.wait_ge(area_free[4], c.at("area4"))
                    swap(3, chunk(mla_m["qr"], 1))
                    values(1)
                    keys(2)
                    values(3)
                    pe.wait_ge(area_free[3], c.at("area3"))
                    attention(half)

                base = c.now("area4") - (H - 1)
                for g in range(2):
                    def heads(kp):
                        pe.wait_ge(area_free[4], base + 2 * kp + 2)
                    square_group((0, 1) if g == 0 else (2, 3), OHI, OLO, heads if g == 0 else anything,
                                 {1: lambda: transposes(HALF_HEADS - 1), 2: lambda: weighted(HALF_HEADS - 1)}
                                 if g == 0 else None)

            def lru():
                square_group((0, 1), HI, LO, h_chunks, {3: token_sums(2, ssq, 7)})
                c.add("h", 8)
                jobs["xb", 0], jobs["xb", 1] = c.now("area0"), c.now("area1")
                spread(2)
                square_group((3, 2), HI, LO, anything)
                jobs["xb", 3], jobs["xb", 2] = c.now("area3"), c.now("area2")

                def gates(half):
                    next_unit_ready()
                    wh, wl = unit()
                    for n in range(4):
                        k = 4 * half + n
                        claim(n % 2)
                        pe.wait_ge(xc_ready, k + 1)
                        for b in range(2):
                            at = slice(b * T + n * P, b * T + (n + 1) * P)
                            mm = product(bank(n % 2, b), (wh[:, at], wl[:, at]), (UHI[k], ULO[k]), True, True)
                        if n < 3:
                            mm.then_inc(psum_done, 1)
                            c.add("psum_done")
                    mm.then_inc(unit_done, 1)
                    c.add("tensor_unit")

                jobs["gates", 0], jobs["gates", 1] = c.now("area0"), c.now("area1")
                gates(0)
                square_group((2, 3), HI, LO, anything)
                jobs["gate", 0] = c.now("area2"), c.now("area3")
                gates(1)
                square_group((2, 3), HI, LO, anything)
                jobs["gate", 1] = c.now("area2"), c.now("area3")
                down(0)
                down(1)

            def swa():
                def swaps(a, p):
                    def run():
                        pe.wait_ge(biased, 2 if p == 4 else 2 * p + 4)
                        claim(a)
                        for b in range(2):
                            mm = swap_rows(bank(a, b), 1, chunk(swa_m["q"], 2 * p + b) if p < 4
                                           else chunk(swa_m["p"], b))
                        mm.then_inc(psum_done, 1)
                        c.add("psum_done")
                    return run

                hooks = {1: rotary_angles(1), 3: token_sums(2, ssq, 7)}
                claim(0)
                claim(1)
                jobs["k"] = c.now("area0")
                for kp in range(4):
                    if kp in hooks:
                        hooks[kp]()
                    h_chunks(kp)
                    next_unit_ready()
                    wh, wl = unit()
                    for kk in range(2):
                        k = 2 * kp + kk
                        for m in range(2):
                            at = slice(kk * T + m * P, kk * T + (m + 1) * P)
                            mm = product(bank(0, m), (wh[:, at], wl[:, at]), (HI[k], LO[k]), k == 0, k == KC - 1)
                        for t in range(QB):
                            tok = slice(t * P, (t + 1) * P)
                            at = slice(kk * T + 256, kk * T + 512)
                            mm = product(area(1)[:, t * 256:(t + 1) * 256], (HI[k][:, tok], LO[k][:, tok]),
                                         (wh[:, at], wl[:, at]), k == 0 and t % 2 == 0, k == KC - 1, skip=True)
                    mm.then_inc(unit_done, 1)
                    c.add("tensor_unit")
                c.add("h", 8)
                spread(2)
                square_group((3, 2), HI, LO, anything, {2: swaps(0, 4)})
                jobs["q", 0], jobs["q", 1] = c.now("area3"), c.now("area2")
                square_group((0, 1), HI, LO, anything, {2: swaps(2, 0), 3: swaps(3, 1)})
                jobs["q", 2], jobs["q", 3] = c.now("area0"), c.now("area1")

                def scores(i, half):
                    claim(half)
                    for b in (2 * half, 2 * half + 1):
                        for a in range(2):
                            rows = slice(64 * a, 64 * a + 64)
                            n = 256 if b else 128
                            mm = nc.tensor.matmul(bank(half, a)[:, b % 2 * 256:b % 2 * 256 + n],
                                                  chunk(swa_m["q"], i)[rows, b * P:(b + 1) * P],
                                                  chunk(swa_m["kd"], i // 2)[rows, (b + 1) * P - n:(b + 1) * P],
                                                  start=True, stop=True, skip_group_check=True)
                    mm.then_inc(psum_done, 1)
                    c.add("psum_done")

                def transposes(i, last_area=1):
                    c.add("p")
                    pe.wait_ge(p_ready, c.now("p"))
                    p = swa_m["p"][:, (i % 2) * W_ATT:(i % 2 + 1) * W_ATT]
                    for ar, tiles in ((2, (0, 1)), (3, (2,)), (last_area, (3,))):
                        claim(ar)
                        at = 0
                        for j in tiles:
                            for a in range(2):
                                for b in (j, j + 1):
                                    if b < QB:
                                        off = a * P if b == 0 else 256 + (b - 1) * 512 + a * 256 + (j - b + 1) * P
                                        mm = nc.tensor.transpose(area(ar)[:, at:at + P], p[:, off:off + P], ident)
                                        at += P
                        mm.then_inc(psum_done, 1)
                        c.add("psum_done")

                def weighted(i):
                    pe.wait_ge(area_free[2], c.at("area2"))
                    pe.wait_ge(area_free[3], c.at("area3"))
                    claim(4)
                    for a in range(2):
                        for j in range(QB):
                            n = 256 if j < 3 else 128
                            at = j * 512 + a * n
                            v_at = j * 256 + (i // 2) * 64
                            mm = nc.tensor.matmul(bank(3, 1)[64 * a:64 * a + 64, j * P:j * P + n],
                                                  swa_m["v"][:, v_at:v_at + 64], swa_m["pt"][:, at:at + n],
                                                  start=j == 0, stop=j == 3, skip_group_check=True)
                    mm.then_inc(psum_done, 1)
                    c.add("psum_done")

                for i in range(KC):
                    if i in (0, 4):
                        pe.wait_ge(mixed, 3 if i == 0 else 5)
                    scores(i, 0)
                    scores(i, 1)
                    if i == 0:
                        swaps(2, 2)()
                        swaps(3, 3)()
                    if i >= 2:
                        weighted(i - 2)
                    if i >= 1:
                        transposes(i - 1)
                base = c.now("area4") - (KC - 2)

                def last_but_one():
                    weighted(KC - 2)
                    transposes(KC - 1, 2)

                for g in range(2):
                    def heads(kp):
                        pe.wait_ge(area_free[4], base + 2 * kp + 2)
                    square_group((0, 1) if g == 0 else (2, 3), UHI, ULO, heads if g == 0 else anything,
                                 {1: last_but_one, 2: lambda: weighted(KC - 1)} if g == 0 else None)

            pe.wait_ge(ones_set, 1)
            for kind, i in PHASES:
                if kind == "mla":
                    mla(i)
                elif kind == "mlp":
                    mlp()
                elif kind == "lru":
                    lru()
                elif kind == "swa":
                    swa()
                else:
                    claim(2)
                    before = 8 * (len(PHASES) - 1) + 5 * sum(k == "mla" for k, _ in PHASES)
                    for n, source in enumerate([ssq] + late_squares):
                        if n == 0:
                            pe.wait_ge(squares_added, c.now("squares_added") + 3)
                        else:
                            pe.wait_ge(squares, before + 4 + n)
                        for t in range(QB):
                            mm = nc.tensor.matmul(bank(2)[:, t:t + 1], source[:, t * P:(t + 1) * P], ones[:, 0:1],
                                                  start=n == 0 and t == 0, stop=n == len(late_squares),
                                                  skip_group_check=True)
                    mm.then_inc(psum_done, 1)
                    c.add("psum_done")
                    spread(2)
                passed.append(dict(c.n))

        @block.vector
        def _(dve):
            c = Counts()

            def link(ins):
                ins.then_inc(vec_step, 1)
                c.add("vec_step")
                dve.wait_ge(vec_step, c.now("vec_step"))

            def free(ins, a):
                ins.then_inc(area_free[a], 1)
                c.add(f"area{a}")

            def exact(t):
                return t.bitcast(F32)

            def split(n):
                for _ in range(n):
                    if c.now("unit") == len(units):
                        return
                    at = c.now("unit") % SLOTS * UNIT
                    to = slice(at, at + units[c.now("unit")][-1])
                    dve.wait_ge(w_hi_done, c.at("unit", 1))
                    nc.vector.tensor_tensor(w_lo[:, to], w_raw[:, to], exact(w_hi[:, to]), ALU.subtract
                                            ).then_inc(w_ready, 1)
                    c.add("unit")

            def sum_ready():
                c.add("psum_done")
                dve.wait_ge(psum_done, c.at("psum_done"))

            def units_passed(n):
                c.add("tensor_unit", n)
                dve.wait_ge(unit_done, c.at("tensor_unit"))

            def prepare(p, gain):
                for k in (2 * p, 2 * p + 1):
                    c.add("h")
                    c.add("squares")
                    dve.wait_ge(h_hi_done, c.now("h"))
                    nc.vector.scalar_tensor_tensor(out=LO[k], in0=chunk(x, k), scalar=col(*gain(k)),
                                                   in1=exact(HI[k]), op0=ALU.mult, op1=ALU.subtract
                                                   ).then_inc(h_ready, 1)

            def newton(out, r, v, t, scale=1.0):
                link(nc.vector.tensor_tensor(t, r, r, ALU.mult))
                link(nc.vector.tensor_tensor(t, t, v, ALU.mult))
                link(nc.vector.tensor_scalar(t, t, -0.5 * scale, 1.5 * scale, ALU.mult, ALU.add))
                link(nc.vector.tensor_tensor(out, r, t, ALU.mult))

            def root_ready():
                c.add("root")
                dve.wait_ge(root_done, c.now("root"))

            def norm_rows():
                sum_ready()
                root_ready()
                free(nc.vector.tensor_scalar(var[:, :], bank(2), 1.0 / D, EPS, ALU.mult, ALU.add), 2)
                link(nc.vector.reciprocal(root[:, :], root[:, :]))
                newton(rstd[:, :], root[:, :], var[:, :], rstd2[:, :])
                link(nc.vector.tensor_tensor(rstd2[:, :], rstd[:, :], rstd[:, :], ALU.mult))

            def norm_columns(out, a, n, inner=False, scale=1.0):
                sum_ready()
                if inner:
                    free(nc.vector.scalar_tensor_tensor(out=var4, in0=bank(a)[:, 0:QB], scalar=1.0 / n, in1=rstd2_4,
                                                        op0=ALU.mult, op1=ALU.mult), a)
                else:
                    free(nc.vector.tensor_scalar(var4, bank(a)[:, 0:QB], 1.0 / n, None, ALU.mult), a)
                dve.wait_ge(area_free[a], c.at(f"area{a}"))
                nc.vector.tensor_scalar(var4, var4, EPS, None, ALU.add).then_inc(var_ready, 1)
                root_ready()
                link(nc.vector.reciprocal(root4, root4))
                newton(out, root4, var4, step4, scale)
                if inner:
                    link(nc.vector.tensor_tensor(out, out, rstd4, ALU.mult))
                dve.wait_ge(const_loaded, 32)
                nc.vector.tensor_tensor(diag[:, :].rearrange("p (b n) -> p b n", b=QB),
                                        ident.unsqueeze(1).to_broadcast([P, QB, P]),
                                        out.unsqueeze(2).to_broadcast([P, QB, P]), ALU.mult).then_inc(diag_ready, 1)
                if not inner:
                    link(nc.vector.tensor_tensor(rstd2_4, rstd4, rstd4, ALU.mult))

            def spread_in(to, a=2):
                sum_ready()
                free(nc.vector.tensor_copy(to, bank(a)), a)
                dve.wait_ge(area_free[a], c.at(f"area{a}"))

            def tables_made():
                c.add("psum_done")
                c.add("area3")
                return c.now("area3")

            def squared_relu(g):
                a = 2 * g
                for q in range(2):
                    c.add(f"area{a + q}")
                    dve.wait_ge(area_free[a + q], c.at(f"area{a + q}"))
                    r = chunk(mlp_m["relu"], 2 * q, 2)
                    nc.vector.tensor_tensor(r, r, r, ALU.mult).then_inc(squared, 1)
                for q in range(2):
                    c.add("u_hi")
                    dve.wait_ge(u_hi_done, c.at("u_hi"))
                    nc.vector.tensor_tensor(chunk(u_lo, 2 * (a + q), 2), chunk(mlp_m["relu"], 2 * q, 2),
                                            exact(chunk(u_hi, 2 * (a + q), 2)), ALU.subtract).then_inc(u_ready, 1)
                c.add("psum_done")
                c.add("tensor_unit", 4)

            def add_scaled(g):
                for q in range(2):
                    a = 2 * g + q
                    if q == 0:
                        sum_ready()
                    else:
                        units_passed(4)
                    free(nc.vector.tensor_tensor(two(chunk(mlp_m["scaled"], 2 * q, 2)), two(area(a)),
                                                 twice(rstd2[:, :]), ALU.mult), a)
                    dve.wait_ge(area_free[a], c.at(f"area{a}"))
                    nc.vector.tensor_tensor(chunk(x, 2 * a, 2), chunk(x, 2 * a, 2), chunk(mlp_m["scaled"], 2 * q, 2),
                                            ALU.add).then_inc(x_ready, 1)

            def mlp(gain):
                split(3)
                norm_rows()
                split(1)
                with dve.Fori(0, TURNS) as turn:
                    c.begin(turn)
                    squared_relu(0)
                    split(4)
                    squared_relu(1)
                    split(4)
                    add_scaled(0)
                    split(4)
                    add_scaled(1)
                    split(4)
                    c.end(TURNS)
                squared_relu(0)
                split(4)
                squared_relu(1)
                split(4)
                for g in range(2):
                    add_scaled(g)
                    if gain:
                        prepare(2 * g, gain)
                        prepare(2 * g + 1, gain)
                    split(3 if g == 0 else 1)

            def add_product(gain, bias=None):
                for g in range(2):
                    for q in range(2):
                        a = 2 * g + q
                        if q == 0:
                            sum_ready()
                        else:
                            units_passed(4)
                        if bias is None:
                            free(nc.vector.tensor_tensor(chunk(x, 2 * a, 2), chunk(x, 2 * a, 2), area(a), ALU.add), a)
                        else:
                            for b in range(2):
                                k = 2 * a + b
                                add = nc.vector.scalar_tensor_tensor(out=chunk(x, k), in0=bank(a, b),
                                                                     scalar=col(bias, k), in1=chunk(x, k),
                                                                     op0=ALU.add, op1=ALU.add)
                            free(add, a)
                    prepare(2 * g, gain)
                    prepare(2 * g + 1, gain)
                    split(3 if g == 0 else 1)

            def rotate(rows, swapped, a, scratch, wide=False):
                f = two if wide else (lambda t: t)
                tab = (lambda t: twice(t[:, :])) if wide else (lambda t: t[:, :])
                free(nc.vector.tensor_tensor(f(scratch), f(swapped), tab(sin), ALU.mult), a)
                link(nc.vector.tensor_tensor(f(rows), f(rows), tab(cos), ALU.mult))
                if not wide:
                    link(nc.vector.tensor_tensor(rows, rows, scratch, ALU.add))

            kraw = swa_m["p"][:, 0:PAIR]
            nmax = small[:, 0:16]
            total = small[:, 16:32]
            inverse = small[:, 32:48]
            sink_part = small[:, 48:64]

            def head_lo(o_hi, o_lo):
                c.add("psum_done")
                c.add("o_hi")
                dve.wait_ge(o_hi_done, c.now("o_hi"))
                free(nc.vector.tensor_tensor(o_lo, bank(3, 1), exact(o_hi), ALU.subtract), 4)

            def mla(j, gain):
                split(3)
                tables = tables_made()
                norm_columns(rstd4, 2, D)
                split(1)

                def lo(t, a, b):
                    g = col("q_norm", 3 * j + t) if t < 3 else col("kv_norm", 2 * j + t - 3)
                    c.add("u_hi")
                    dve.wait_ge(u_hi_done, c.now("u_hi"))
                    return nc.vector.scalar_tensor_tensor(out=ULO[t], in0=bank(a, b), scalar=g, in1=exact(UHI[t]),
                                                          op0=ALU.mult, op1=ALU.subtract)
                c.add("psum_done")
                c.add("tensor_unit", 4)
                for t in range(4):
                    ins = lo(t, t // 2, t % 2)
                    if t % 2:
                        free(ins, t // 2)
                    if t == 1:
                        spread_in(rstd[:, :])
                norm_columns(token_scale, 2, QL, inner=True, scale=SCALE)
                units_passed(2)
                nc.vector.tensor_tensor(mla_m["kr"], bank(3, 1), rstd[:, :], ALU.mult).then_inc(rows_ready, 1)
                free(lo(4, 3, 0), 3)
                spread_in(mla_m["rq"])
                split(2)
                rope = mla_m["pt"][:, 0:T]

                def nope_queries(n, a):
                    free(nc.vector.tensor_tensor(two(chunk(mla_m["qn"], 2 * n, 2)), two(area(a)), twice(mla_m["rq"]),
                                                 ALU.mult), a)

                def rotary_queries(n, a):
                    nc.vector.tensor_tensor(chunk(mla_m["qr"], n), bank(a), mla_m["rq"], ALU.mult
                                            ).then_inc(rows_ready, 1)

                def finish(n, a, wait=True):
                    if wait:
                        sum_ready()
                    rotate(chunk(mla_m["qr"], n), bank(a, 1), a, rope)

                def keys(n, a):
                    sum_ready()
                    free(nc.vector.tensor_tensor(two(chunk(mla_m["kn"], 2 * n, 2)), two(area(a)), twice(mla_m["rkv"]),
                                                 ALU.mult), a)

                def values(n, a):
                    units_passed(1)
                    out = mla_m["v"].rearrange("p (t n) -> p t n", t=QB)[:, :, n * 256:(n + 1) * 256]
                    free(nc.vector.tensor_tensor(out, area(a).rearrange("p (t n) -> p t n", t=QB),
                                                 token_scale.unsqueeze(2).to_broadcast([P, QB, 256]), ALU.mult), a)

                def attention(half):
                    for i in range(HALF_HEADS + 1):
                        at = 4 * (i % 2)
                        if i < HALF_HEADS:
                            for a, blocks in ((0, (3, 2)), (1, (1, 0))):
                                sum_ready()
                                off = 0 if a == 0 else 896
                                for b in blocks:
                                    edge = S_OFF[b] - off + P * b + CHUNK
                                    ins = nc.vector.memset(area(a)[0:CHUNK, edge:edge + CHUNK], NEG)
                                link(ins)
                                for b in blocks:
                                    s = area(a)[:, S_OFF[b] - off:S_OFF[b] - off + P * (b + 1)]
                                    ins = nc.vector.tensor_reduce(nmax[:, at + b:at + b + 1], s, AX.X, ALU.max,
                                                                  negate=True)
                                ins.then_inc(nmax_ready, 1)
                                c.add(f"area{a}")
                        if i >= 2:
                            h = half * HALF_HEADS + i - 2
                            head_lo(OHI[h], OLO[h])
                        if i >= 1:
                            c.add("psum_done")
                            c.add("area2")
                            sum_ready()
                            free(nc.vector.tensor_copy(mla_m["pt"][:, 896:ATT], area(3)[:, 0:384]), 3)
                        if i < HALF_HEADS:
                            dve.wait_ge(area_free[1], c.at("area1"))
                            link(nc.vector.reciprocal(inverse[:, at:at + 4], total[:, at:at + 4]))
                            for b in range(QB):
                                p = mla_m["p"][:, (i % 2) * ATT + S_OFF[b]:(i % 2) * ATT + S_OFF[b] + P * (b + 1)]
                                ins = nc.vector.tensor_scalar(p, p, inverse[:, at + b:at + b + 1], None, ALU.mult)
                            ins.then_inc(p_ready, 1)

                for half in range(2):
                    sum_ready()
                    if half == 0:
                        sum_ready()
                        dve.wait_ge(area_free[3], tables)
                        rotate(mla_m["kr"], bank(2, 1), 2, rope)
                        norm_columns(token_scale, 3, KVL, inner=True)
                    nope_queries(0, 0)
                    units_passed(1)
                    rotary_queries(0, 1)
                    if half == 1:
                        head_lo(OHI[HALF_HEADS - 1], OLO[HALF_HEADS - 1])
                    split(1)
                    sum_ready()
                    nope_queries(1, 2)
                    units_passed(1)
                    rotary_queries(1, 3)
                    split(1)
                    if half == 0:
                        c.add("psum_done", 2)
                        dve.wait_ge(psum_done, c.now("psum_done"))
                        link(nc.vector.tensor_copy(mla_m["rkv"], bank(1)))
                    finish(0, 1, wait=half == 1)
                    keys(0, 0)
                    finish(1, 3)
                    values(0, 1)
                    keys(1, 2)
                    values(1, 3)
                    split(2)
                    attention(half)
                head_lo(OHI[H - 1], OLO[H - 1])
                split(4)
                add_product(gain)

            def softplus_of_lambda():
                e, z, z2, s, m = (small[:, 8 * n:8 * n + 8] for n in range(1, 6))
                dve.wait_ge(lam_exp, 1)
                link(nc.vector.tensor_scalar(s, e, 2.0, None, ALU.add))
                link(nc.vector.reciprocal(s, s))
                link(nc.vector.tensor_tensor(z, e, s, ALU.mult))
                link(nc.vector.tensor_tensor(z2, z, z, ALU.mult))
                link(nc.vector.tensor_scalar(s, z2, 1.0 / 17, None, ALU.mult))
                for d in (15, 13, 11, 9, 7, 5, 3):
                    link(nc.vector.scalar_tensor_tensor(out=s, in0=s, scalar=1.0 / d, in1=z2, op0=ALU.add,
                                                        op1=ALU.mult))
                link(nc.vector.scalar_tensor_tensor(out=s, in0=s, scalar=1.0, in1=z, op0=ALU.add, op1=ALU.mult))
                link(nc.vector.tensor_scalar(m, col("lambda", 0, 8), -1.0, 0.0, ALU.mult, ALU.max))
                link(nc.vector.scalar_tensor_tensor(out=s, in0=s, scalar=2.0, in1=m, op0=ALU.mult, op1=ALU.add))
                link(nc.vector.tensor_scalar(sp4, s, 4.0, None, ALU.mult))
                nc.vector.tensor_scalar(spm8, s, -8.0, None, ALU.mult).then_inc(softplus, 1)

            def lru(gain):
                m = lru_m
                softplus_of_lambda()
                split(3)
                norm_columns(rstd4, 2, D)
                split(1)
                for n in range(4):
                    ins = nc.vector.memset(pads[n][:, 0:3], 0.0)
                link(ins)

                def fill_pads(g):
                    for k in range(4 * g, 4 * g + 4):
                        if k == 0:
                            sum_ready()
                            c.add("tensor_unit", 4)
                            spread_in(rstd[:, :])
                        elif k == 4:
                            sum_ready()
                        elif k == 6:
                            units_passed(4)
                        a = (0, 1, 3, 2)[k // 2]
                        ins = nc.vector.tensor_tensor(pads[k % 4][:, 3:], bank(a, k % 2), rstd[:, :], ALU.mult)
                        if k % 2:
                            free(ins, a)
                    dve.wait_ge(area_free[a], c.at(f"area{a}"))

                def conv(k):
                    pad, out = pads[k % 4], chunk(m["xc"], k)
                    dve.wait_ge(tap_done, k + 1)
                    for w in range(1, 4):
                        ins = nc.vector.scalar_tensor_tensor(out=out, in0=pad[:, w:w + T], scalar=col("conv_w", 8 * w + k),
                                                             in1=out, op0=ALU.mult, op1=ALU.add)
                        if w < 3:
                            link(ins)
                    ins.then_inc(xc_done, 1)

                def xc_lo(k):
                    dve.wait_ge(xc_hi_done, k + 1)
                    nc.vector.tensor_tensor(ULO[k], chunk(m["xc"], k), exact(UHI[k]), ALU.subtract
                                            ).then_inc(xc_ready, 1)

                def gate_in(g):
                    for q in range(2):
                        if q == 0:
                            sum_ready()
                        else:
                            units_passed(4)
                        free(nc.vector.tensor_tensor(two(gate[2 * g + q]), two(area(2 + q)),
                                                     twice(rstd[:, :]), ALU.mult), 2 + q)

                def decay(k):
                    r, i, t = rit[k % 4]
                    dve.wait_ge(decay_in, k + 1)
                    ins = nc.vector.scalar_tensor_tensor(out=r, in0=r, scalar=1.0, in1=t, op0=ALU.add, op1=ALU.mult)
                    ins.then_inc(decay_used, 1)
                    dve.wait_ge(decay_used, k + 1)
                    link(nc.vector.tensor_scalar(r, r, -1.0, 1.0, ALU.mult, ALU.add))

                def recurrence(k):
                    r, i, t = rit[k % 4]
                    dve.wait_ge(roots, k + 1)
                    link(nc.vector.scalar_tensor_tensor(out=t, in0=r, scalar=1.0, in1=t, op0=ALU.add, op1=ALU.mult))
                    dve.wait_ge(gated, k + 1)
                    link(nc.vector.tensor_tensor(i, i, t, ALU.mult))
                    nc.vector.tensor_tensor_scan(chunk(m["xc"], k), r, i, 0.0, ALU.mult, ALU.add).then_inc(scanned, 1)
                    dve.wait_ge(scanned, k + 1)

                def gates_passed():
                    c.add("psum_done", 3)
                    c.add("tensor_unit")
                    c.add("area0", 2)
                    c.add("area1", 2)

                def y(p):
                    c.add("gate")
                    dve.wait_ge(gate_done, c.now("gate"))
                    g = gate[p]
                    nc.vector.tensor_tensor(g, g, chunk(m["xc"], 2 * p, 2), ALU.mult).then_inc(y_done, 1)

                def y_lo(p):
                    c.add("u_hi")
                    dve.wait_ge(u_hi_done, c.now("u_hi"))
                    nc.vector.tensor_tensor(chunk(u_lo, 2 * p, 2), gate[p],
                                            exact(chunk(u_hi, 2 * p, 2)), ALU.subtract).then_inc(u_ready, 1)

                fill_pads(0)
                for k in range(4):
                    conv(k)
                    if k:
                        xc_lo(k - 1)
                split(2)
                xc_lo(3)
                split(1)
                fill_pads(1)
                split(1)
                gates_passed()
                conv(4)
                conv(5)
                xc_lo(4)
                split(1)
                decay(0)
                decay(1)
                xc_lo(5)
                conv(6)
                decay(2)
                decay(3)
                split(1)
                recurrence(0)
                recurrence(1)
                xc_lo(6)
                split(1)
                conv(7)
                recurrence(2)
                xc_lo(7)
                gate_in(0)
                recurrence(3)
                gates_passed()
                split(2)
                decay(4)
                decay(5)
                decay(6)
                decay(7)
                y(0)
                y(1)
                recurrence(4)
                y_lo(0)
                split(1)
                recurrence(5)
                y_lo(1)
                split(1)
                recurrence(6)
                split(1)
                recurrence(7)
                gate_in(1)
                split(1)
                y(2)
                y(3)
                y_lo(2)
                y_lo(3)
                split(5)
                add_product(gain)

            def swa(gain):
                m = swa_m
                scratch = m["p"][:, 2 * PAIR:3 * PAIR]
                split(3)
                tables = tables_made()
                norm_columns(rstd4, 2, D)
                split(1)

                def rows_in(g):
                    sum_ready()
                    for q in range(2):
                        if q:
                            units_passed(4)
                        a = 3 - q if g == 0 else q
                        free(nc.vector.tensor_tensor(two(chunk(m["q"], 4 * g + 2 * q, 2)), two(area(a)),
                                                     twice(rstd[:, :]), ALU.mult), a)

                def rotate_queries(p, a):
                    sum_ready()
                    q = chunk(m["q"], 2 * p, 2)
                    rotate(q, area(a), a, scratch, wide=True)
                    nc.vector.tensor_tensor(q, q, scratch, ALU.add).then_inc(mixed, 1)

                c.add("tensor_unit", 4)
                spread_in(rstd[:, :])
                free(nc.vector.tensor_tensor(two(kraw), two(area(0)), twice(rstd[:, :]), ALU.mult), 0)
                dve.wait_ge(extra_loaded, 32)
                for t in range(QB):
                    ins = nc.vector.scalar_tensor_tensor(out=m["v"][:, t * 256:(t + 1) * 256],
                                                         in0=area(1)[:, t * 256:(t + 1) * 256],
                                                         scalar=rstd4[:, t:t + 1], in1=m["bv"],
                                                         op0=ALU.mult, op1=ALU.add)
                free(ins, 1)
                split(2)
                dve.wait_ge(area_free[3], tables)
                sum_ready()
                rotate(kraw, area(0), 0, scratch, wide=True)
                for g in range(SW_G):
                    src = slice(64 * (g % 2), 64 * (g % 2) + 64)
                    for half in range(2):
                        ins = nc.vector.tensor_tensor(chunk(m["kd"], g)[64 * half:64 * half + 64, :],
                                                      chunk(kraw, g // 2)[src, :], chunk(scratch, g // 2)[src, :],
                                                      ALU.add)
                ins.then_inc(mixed, 1)
                dve.wait_ge(mixed, 1)
                split(1)
                rows_in(0)
                split(3)
                rotate_queries(0, 2)
                split(1)
                dve.wait_ge(mixed, 2)
                rotate_queries(1, 3)
                rows_in(1)
                dve.wait_ge(mixed, 3)

                mask = const[:, C_MASK:C_MASK + 256]
                for i in range(KC + 1):
                    at = 8 * (i % 2)
                    p = m["p"][:, (i % 2) * W_ATT:(i % 2 + 1) * W_ATT]

                    def blocks(b):
                        n = 256 if b else 128
                        return n, (0 if b == 0 else 256 + (b - 1) * 512)

                    def masked(half):
                        sum_ready()
                        for b in (2 * half, 2 * half + 1):
                            n, off = blocks(b)
                            for a in range(2):
                                ins = nc.vector.tensor_tensor_reduce(
                                    out=p[:, off + a * n:off + (a + 1) * n],
                                    in0=bank(half, a)[:, b % 2 * 256:b % 2 * 256 + n],
                                    in1=mask[:, 256 - n:256], scale=SW_D ** -0.5,
                                    scalar=m["sinks"][:, 2 * i + a:2 * i + a + 1], op0=ALU.add, op1=ALU.max,
                                    accum_out=nmax[:, at + 2 * b + a:at + 2 * b + a + 1])
                        free(ins, half)

                    def normalised(i):
                        c.add("exp")
                        dve.wait_ge(exp_done, c.now("exp"))
                        s8 = slice(8 * (i % 2), 8 * (i % 2) + 8)
                        link(nc.vector.tensor_tensor(total[:, s8], total[:, s8], sink_part[:, s8], ALU.add))
                        link(nc.vector.reciprocal(inverse[:, s8], total[:, s8]))
                        for b in range(QB):
                            n, off = blocks(b)
                            for a in range(2):
                                at = (i % 2) * W_ATT + off + a * n
                                q = m["p"][:, at:at + n]
                                k = 8 * (i % 2) + 2 * b + a
                                ins = nc.vector.tensor_scalar(q, q, inverse[:, k:k + 1], None, ALU.mult)
                        ins.then_inc(p_ready, 1)

                    if i == 1:
                        normalised(0)
                    if i < KC:
                        masked(0)
                    if 2 <= i <= KC:
                        normalised(i - 1)
                    if i < KC:
                        masked(1)
                        dve.wait_ge(area_free[1], c.at("area1"))
                        nm = nmax[:, at:at + 8]
                        link(nc.vector.tensor_scalar(nm, nm, -1.0, None, ALU.mult))
                        nc.vector.tensor_tensor(sink_part[:, at:at + 8].rearrange("p (b a) -> p b a", a=2),
                                                nm.rearrange("p (b a) -> p b a", a=2),
                                                m["sinks"][:, 2 * i:2 * i + 2].unsqueeze(1).to_broadcast([P, QB, 2]),
                                                ALU.add).then_inc(nmax_ready, 1)
                    if i == 0:
                        rotate_queries(2, 2)
                        dve.wait_ge(mixed, 4)
                        rotate_queries(3, 3)
                        dve.wait_ge(mixed, 5)
                        split(1)
                    if i >= 2:
                        head_lo(UHI[i - 2], ULO[i - 2])
                    if 1 <= i <= KC:
                        sum_ready()
                        free(nc.vector.tensor_copy(m["pt"][:, 0:PAIR], area(2)), 2)
                        c.add("psum_done")
                        c.add("area3")
                        sum_ready()
                        a = 1 if i < KC else 2
                        free(nc.vector.tensor_copy(m["pt"][:, PAIR + T:W_ATT], area(a)[:, 0:W_ATT - PAIR - T]), a)
                head_lo(UHI[KC - 1], ULO[KC - 1])
                split(4)
                add_product(gain, "swa_b_o")

            def final():
                dve.wait_ge(x_ready, 4 * SLICES * sum(k == "mlp" for k, _ in PHASES))
                for k in range(KC):
                    ins = nc.vector.tensor_scalar(chunk(arena, k), chunk(x, k), col("norm_final", k), None, ALU.mult)
                link(ins)
                norm_columns(rstd4, 2, D)
                sum_ready()
                c.add("area2")
                for p in range(KC // 2):
                    t = two(chunk(arena, 2 * p, 2))
                    nc.vector.tensor_tensor(t, t, twice(bank(2)), ALU.mult).then_inc(out_ready, 1)

            dve.wait_ge(cols_loaded, 16)
            for p in range(4):
                prepare(p, gains(-1))
                split(1)
            for n, (kind, i) in enumerate(PHASES):
                if kind == "final":
                    final()
                else:
                    {"mla": lambda g: mla(i, g), "mlp": mlp, "lru": lru, "swa": swa}[kind](gains(n))
                for name in ("psum_done", "tensor_unit", "area0", "area1", "area2", "area3", "area4"):
                    assert c.now(name) == passed[n].get(name, 0), (kind, i, name, c.now(name), passed[n])

        @block.scalar
        def _(act):
            c = Counts()
            some = slice(C_FREQ, C_PICK)
            load_positions(act)
            act.dma_start(const[:, some], A["const"][:, some]).then_inc(freq_loaded, 16)
            act.wait_ge(cols_loaded, 16)

            def link(ins):
                ins.then_inc(act_step, 1)
                c.add("act_step")
                act.wait_ge(act_step, c.now("act_step"))

            def split(n):
                for _ in range(n):
                    if c.now("unit") == len(units):
                        return
                    u = units[c.now("unit")]
                    slot = c.now("unit") % SLOTS
                    to = slice(slot * UNIT, slot * UNIT + u[-1])
                    c.add(f"loaded{slot}", 16 * LOADS.get(u[0], 1))
                    act.wait_ge(w_loaded[slot], c.at(f"loaded{slot}"))
                    need(act, unit_done, c.at("unit", 1 - SLOTS))
                    nc.scalar.activation(w_hi[:, to], w_raw[:, to], ACT.Copy).then_inc(w_hi_done, 1)
                    c.add("unit")

            def sum_ready():
                c.add("psum_done")
                act.wait_ge(psum_done, c.at("psum_done"))

            def units_passed(n):
                c.add("tensor_unit", n)
                act.wait_ge(unit_done, c.at("tensor_unit"))

            def prepare(p, gain, ready, first=False):
                ready(p)
                pair = (2 * p, 2 * p + 1)
                if gain:
                    for k in pair:
                        nc.scalar.activation(HI[k], chunk(x, k), ACT.Copy, scale=col(*gain(k))).then_inc(h_hi_done, 1)
                for k in pair:
                    if k == 0:
                        to = ssq[:, :]
                    elif first:
                        to = chunk(arena, k)
                    elif not gain and k >= 4:
                        to = late_squares[k - 4]
                    else:
                        to = chunk(sq, k % 2)
                        if k >= 3:
                            act.wait_ge(squares_added, c.now("squares_added") + k - 2)
                    nc.scalar.activation(to, chunk(x, k), ACT.Square).then_inc(squares, 1)
                if p == 3:
                    c.add("squares_added", 7)

            def norm_root():
                sum_ready()
                nc.scalar.activation(root[:, :], bank(2), ACT.Sqrt, bias=eps_col, scale=1.0 / D).then_inc(root_done, 1)

            def column_root():
                c.add("psum_done")
                c.add("var")
                act.wait_ge(var_ready, c.now("var"))
                nc.scalar.activation(root4, var4, ACT.Sqrt).then_inc(root_done, 1)

            def spread_passed():
                c.add("psum_done")

            def squared_relu(g):
                a = 2 * g
                for q in range(2):
                    if q == 0:
                        sum_ready()
                    else:
                        units_passed(4)
                    if g == 1:
                        act.wait_ge(u_ready, c.at("u_ready", q - 1))
                    nc.scalar.activation(chunk(mlp_m["relu"], 2 * q, 2), area(a + q), ACT.Relu
                                         ).then_inc(area_free[a + q], 1)
                for q in range(2):
                    c.add("squared")
                    act.wait_ge(squared, c.at("squared"))
                    nc.scalar.activation(chunk(u_hi, 2 * (a + q), 2), chunk(mlp_m["relu"], 2 * q, 2), ACT.Copy
                                         ).then_inc(u_hi_done, 1)
                c.add("u_ready", 2)

            def down_passed():
                c.add("psum_done")
                c.add("tensor_unit", 4)
                c.add("x_ready", 2)

            def mlp(n, gain):
                split(3)
                norm_root()
                split(1)
                with act.Fori(0, TURNS) as turn:
                    c.begin(turn)
                    squared_relu(0)
                    split(4)
                    squared_relu(1)
                    split(4)
                    down_passed()
                    split(4)
                    down_passed()
                    split(4)
                    c.end(TURNS)
                squared_relu(0)
                split(4)
                squared_relu(1)
                split(4)
                for g in range(2):
                    down_passed()

                    def ready(p):
                        act.wait_ge(x_ready, c.now("x_ready") - 1 + p % 2)
                    prepare(2 * g, gain, ready)
                    prepare(2 * g + 1, gain, ready)
                    split(3 if g == 0 else 1)

            def after_mixer(n, gain):
                def ready(p):
                    act.wait_ge(area_free[p], passed[n][f"area{p}"])
                for g in range(2):
                    c.add("psum_done")
                    c.add("tensor_unit", 4)
                    prepare(2 * g, gain, ready)
                    prepare(2 * g + 1, gain, ready)
                    split(3 if g == 0 else 1)

            def rotary_tables(which):
                sum_ready()
                sign = const[:, C_SIGN + which:C_SIGN + which + 1]
                nc.scalar.activation(sin[:, :], bank(3, 0), ACT.Sin, scale=sign)
                nc.scalar.activation(cos[:, :], bank(3, 1), ACT.Sin, scale=TURN).then_inc(area_free[3], 1)

            def head_hi(o_hi):
                sum_ready()
                nc.scalar.activation(o_hi, bank(3, 1), ACT.Copy).then_inc(o_hi_done, 1)

            def mla(n, j, gain):
                split(3)
                rotary_tables(0)
                column_root()
                split(1)
                base = c.now("squares_added")
                c.add("psum_done")
                act.wait_ge(psum_done, c.now("psum_done"))
                for t in range(5):
                    if t == 2:
                        units_passed(4)
                    if t == 4:
                        spread_passed()
                        column_root()
                        units_passed(2)
                        spread_passed()
                        act.wait_ge(squares_added, base + 1)
                    source = bank(t // 2, t % 2) if t < 4 else bank(3)
                    g = col("q_norm", 3 * j + t) if t < 3 else col("kv_norm", 2 * j + t - 3)
                    to = (mla_m["rq"], chunk(sq, 1), chunk(sq, 0), mla_m["rkv"], chunk(sq, 1))[t]
                    nc.scalar.activation(to, source, ACT.Square).then_inc(squares, 1)
                    nc.scalar.activation(UHI[t], source, ACT.Copy, scale=g).then_inc(u_hi_done, 1)
                c.add("squares_added", 3)
                split(2)
                c.add("psum_done", 2)
                column_root()

                def attention(half):
                    for i in range(HALF_HEADS + 1):
                        at = 4 * (i % 2)
                        if i < HALF_HEADS:
                            for a, blocks in ((0, (3, 2)), (1, (1, 0))):
                                c.add("psum_done")
                                c.add("nmax")
                                act.wait_ge(nmax_ready, c.now("nmax"))
                                off = 0 if a == 0 else 896
                                for b in blocks:
                                    n_keys = P * (b + 1)
                                    ins = nc.scalar.activation(
                                        mla_m["p"][:, (i % 2) * ATT + S_OFF[b]:(i % 2) * ATT + S_OFF[b] + n_keys],
                                        area(a)[:, S_OFF[b] - off:S_OFF[b] - off + n_keys], ACT.Exp,
                                        bias=nmax[:, at + b:at + b + 1], accum_out=total[:, at + b:at + b + 1])
                                ins.then_inc(area_free[a], 1)
                        if i >= 2:
                            head_hi(OHI[half * HALF_HEADS + i - 2])
                        if i >= 1:
                            sum_ready()
                            nc.scalar.activation(mla_m["pt"][:, 0:896], area(2)[:, 0:896], ACT.Copy
                                                 ).then_inc(area_free[2], 1)
                            c.add("psum_done")

                for half in range(2):
                    if half == 1:
                        c.add("psum_done")
                        head_hi(OHI[HALF_HEADS - 1])
                    split(4)
                    c.add("psum_done", 6 if half == 0 else 5)
                    c.add("tensor_unit", 4)
                    attention(half)
                head_hi(OHI[H - 1])
                split(4)
                after_mixer(n, gain)

            nmax = small[:, 0:16]
            total = small[:, 16:32]
            sink_part = small[:, 48:64]

            def lru(n, gain):
                m = lru_m
                e, s = small[:, 8:16], small[:, 0:8]
                link(nc.scalar.activation(s, col("lambda", 0, 8), ACT.Abs))
                nc.scalar.activation(e, s, ACT.Exp, scale=-1.0).then_inc(lam_exp, 1)
                split(3)
                column_root()
                split(1)

                def first_tap(k):
                    if k % 2 == 0:
                        a = (0, 1, 3, 2)[k // 2]
                        act.wait_ge(area_free[a], jobs["xb", a])
                    nc.scalar.activation(chunk(m["xc"], k), pads[k % 4][:, 0:T], ACT.Identity,
                                         scale=col("conv_w", k), bias=col("conv_b", k)).then_inc(tap_done, 1)

                def xc_hi(k):
                    act.wait_ge(xc_done, k + 1)
                    nc.scalar.activation(UHI[k], chunk(m["xc"], k), ACT.Copy).then_inc(xc_hi_done, 1)

                def gates(half):
                    for k in range(4 * half, 4 * half + 4):
                        if half and k % 2 == 0:
                            act.wait_ge(scanned, k - 2)
                        if k % 4 == 3:
                            units_passed(1)
                        else:
                            sum_ready()
                        r, i, t = rit[k % 4]
                        nc.scalar.activation(r, bank(k % 2, 0), ACT.Sigmoid, bias=col("b_rgate", k))
                        nc.scalar.activation(i, bank(k % 2, 1), ACT.Sigmoid, bias=col("b_igate", k)
                                             ).then_inc(area_free[k % 2], 1)
                        c.add(f"gates{k % 2}")
                        if k % 2:
                            act.wait_ge(area_free[0], gate_jobs(0, c.now("gates0")))
                            act.wait_ge(area_free[1], gate_jobs(1, c.now("gates1")))
                            for kk in (k - 1, k):
                                r, i, t = rit[kk % 4]
                                nc.scalar.activation(t, r, ACT.Tanh, scale=sp4[:, kk:kk + 1]).then_inc(tanh_done, 1)
                        if k == 5:
                            split(1)

                def rough_decay(half):
                    for k in range(4 * half, 4 * half + 4):
                        act.wait_ge(tanh_done, k + 1)
                        r = rit[k % 4][0]
                        nc.scalar.activation(r, r, ACT.Exp, scale=spm8[:, k:k + 1]).then_inc(decay_in, 1)

                def sqrt(batch):
                    for k in (2 * batch, 2 * batch + 1):
                        act.wait_ge(decay_used, k + 1)
                        t = rit[k % 4][2]
                        nc.scalar.activation(t, t, ACT.Sqrt).then_inc(roots, 1)

                def group_passed():
                    c.add("psum_done")
                    c.add("tensor_unit", 4)

                def gelu(g):
                    for q in range(2):
                        act.wait_ge(area_free[2 + q], jobs["gate", g][q])
                        t = gate[2 * g + q]
                        nc.scalar.activation(t, t, ACT.Gelu_apprx_tanh).then_inc(gate_done, 1)

                def y_hi(p):
                    act.wait_ge(y_done, p + 1)
                    nc.scalar.activation(chunk(u_hi, 2 * p, 2), gate[p], ACT.Copy
                                         ).then_inc(u_hi_done, 1)

                c.add("psum_done")
                spread_passed()
                c.add("tensor_unit", 4)
                for k in range(4):
                    first_tap(k)
                for k in range(4):
                    xc_hi(k)
                split(4)
                c.add("psum_done")
                c.add("tensor_unit", 4)
                first_tap(4)
                first_tap(5)
                act.wait_ge(softplus, 1)
                gates(0)
                first_tap(6)
                first_tap(7)
                split(1)
                xc_hi(4)
                rough_decay(0)
                xc_hi(5)
                split(1)
                sqrt(0)
                sqrt(1)
                xc_hi(6)
                split(1)
                xc_hi(7)
                group_passed()
                gates(1)
                split(1)
                rough_decay(1)
                gelu(0)
                sqrt(2)
                sqrt(3)
                y_hi(0)
                split(1)
                y_hi(1)
                split(3)
                group_passed()
                gelu(1)
                split(1)
                y_hi(2)
                y_hi(3)
                c.add("u_ready", 4)
                split(4)
                after_mixer(n, gain)

            def swa(n, gain):
                m = swa_m
                split(3)
                rotary_tables(1)
                column_root()
                split(1)

                def bias(p, a, job):
                    act.wait_ge(area_free[a], job)
                    for k in (2 * p, 2 * p + 1):
                        t = chunk(m["q"], k) if p < 4 else chunk(m["p"], k % 2)
                        nc.scalar.activation(t, t, ACT.Identity, bias=col("swa_b_qk", k)).then_inc(biased, 1)

                c.add("psum_done", 6)
                c.add("tensor_unit", 12)
                bias(4, 0, jobs["k"])
                split(3)
                bias(0, 3, jobs["q", 0])
                bias(1, 2, jobs["q", 1])
                split(4)
                bias(2, 0, jobs["q", 2])
                bias(3, 1, jobs["q", 3])
                for i in range(KC + 1):
                    at = 8 * (i % 2)
                    if i < KC:
                        c.add("psum_done", 2)
                    if i == 0:
                        c.add("psum_done", 2)
                    if i >= 2:
                        head_hi(UHI[i - 2])
                    if i < KC:
                        c.add("nmax")
                        act.wait_ge(nmax_ready, c.now("nmax"))
                        sp = sink_part[:, at:at + 8]
                        nc.scalar.activation(sp, sp, ACT.Exp)
                        p = m["p"][:, (i % 2) * W_ATT:(i % 2 + 1) * W_ATT]
                        for b in range(QB):
                            n_keys, off = (256, 256 + (b - 1) * 512) if b else (128, 0)
                            for a in range(2):
                                q = p[:, off + a * n_keys:off + (a + 1) * n_keys]
                                k = at + 2 * b + a
                                ins = nc.scalar.activation(q, q, ACT.Exp, bias=nmax[:, k:k + 1],
                                                           accum_out=total[:, k:k + 1])
                        ins.then_inc(exp_done, 1)
                    if i == 0:
                        split(1)
                    if 1 <= i <= KC:
                        c.add("psum_done")
                        sum_ready()
                        nc.scalar.activation(m["pt"][:, PAIR:PAIR + T], bank(3), ACT.Copy).then_inc(area_free[3], 1)
                        c.add("psum_done")
                head_hi(UHI[KC - 1])
                split(4)
                after_mixer(n, gain)

            def gate_jobs(a, k):
                return jobs["gates", a] + k

            act.wait_ge(ones_set, 1)
            for p in range(4):
                def ready(p):
                    act.wait_ge(x_loaded[p], 16)
                prepare(p, gains(-1), ready, first=True)
                split(1)
            for n, (kind, i) in enumerate(PHASES):
                if kind == "final":
                    column_root()
                    spread_passed()
                else:
                    {"mla": lambda g: mla(n, i, g), "mlp": lambda g: mlp(n, g), "lru": lambda g: lru(n, g),
                     "swa": lambda g: swa(n, g)}[kind](gains(n))
                for name in ("psum_done", "tensor_unit"):
                    assert c.now(name) == passed[n].get(name, 0), (kind, i, name, c.now(name), passed[n])

        @block.gpsimd
        def _(pool):
            c = Counts()
            g = nc.gpsimd

            def link(ins):
                ins.then_inc(pool_step, 1)
                c.add("step")
                pool.wait_ge(pool_step, c.now("step"))

            def add_squares(to, source):
                c.add("squares")
                pool.wait_ge(squares, c.now("squares"))
                g.tensor_tensor(to, to, source, ALU.add).then_inc(squares_added, 1)
                c.add("added")
                pool.wait_ge(squares_added, c.now("added"))

            def squares_of_x(first=False, chunks=KC):
                c.add("squares")
                for k in range(1, chunks):
                    add_squares(ssq[:, :], chunk(arena, k) if first else chunk(sq, k % 2))

            def angles(kind):
                ang, head, rest, n, total = (tab_m[k] for k in ("ang", "head", "rest", "n", "sum"))
                parts = turn_parts()

                def times(out, in_, f):
                    link(g.tensor_scalar(out, in_, f, 0.0, ALU.mult, ALU.add))

                def whole_off(t):
                    link(g.tensor_scalar(n, t, 1.0, ROUND, ALU.mult, ALU.add))
                    link(g.tensor_scalar(n, n, 1.0, -ROUND, ALU.mult, ALU.add))
                    link(g.tensor_tensor(t, t, n, ALU.subtract))

                c.add("positions", 16 * QB)
                pool.wait_ge(pos_loaded, c.now("positions"))
                link(g.tensor_copy(ang, tab_m["pos"].bitcast(I32)))
                link(g.tensor_scalar(ang, ang, const[:, C_FREQ + kind:C_FREQ + kind + 1], 0.0, ALU.mult, ALU.add))
                times(head, ang, 4097.0)
                link(g.tensor_tensor(rest, head, ang, ALU.subtract))
                link(g.tensor_tensor(head, head, rest, ALU.subtract))
                link(g.tensor_tensor(rest, ang, head, ALU.subtract))
                times(total, head, parts[0])
                whole_off(total)
                whole_off(total)
                for source, part in ((rest, parts[0]), (head, parts[1])):
                    times(ang, source, part)
                    whole_off(ang)
                    link(g.tensor_tensor(total, total, ang, ALU.add))
                for source, part in ((rest, parts[1]), (head, parts[2]), (rest, parts[2]), (head, parts[3])):
                    times(ang, source, part)
                    link(g.tensor_tensor(total, total, ang, ALU.add))
                whole_off(total)
                link(g.tensor_scalar(rest, total, 1.0, 0.25, ALU.mult, ALU.add))
                whole_off(rest)
                blocks = const[:, C_BLOCK:C_BLOCK + QB].unsqueeze(2).to_broadcast([P, QB, P])
                for name, source in (("wide_sin", total), ("wide_cos", rest)):
                    g.tensor_tensor(tab_m[name].rearrange("p (b n) -> p b n", b=QB),
                                    source.unsqueeze(1).to_broadcast([P, QB, P]), blocks, ALU.mult
                                    ).then_inc(turns_ready, 1)
                c.add("turns", 2)

            g.memset(eps_col, EPS)
            g.memset(ones[:, :], 1.0).then_inc(ones_set, 1)
            pool.wait_ge(freq_loaded, 16)
            angles(0)
            squares_of_x(first=True)
            for n, (kind, i) in enumerate(PHASES):
                if kind == "mla":
                    c.add("squares")
                    add_squares(mla_m["rq"], chunk(sq, 1))
                    add_squares(mla_m["rq"], chunk(sq, 0))
                    c.add("squares")
                    add_squares(mla_m["rkv"], chunk(sq, 1))
                if kind == "lru":
                    for k in range(KC):
                        pool.wait_ge(xc_done, k + 1)
                        pool.wait_ge(tanh_done, k + 1)
                        gate_i = rit[k % 4][1]
                        g.tensor_tensor(gate_i, gate_i, chunk(lru_m["xc"], k), ALU.mult).then_inc(gated, 1)
                if kind == "mlp" and before_rotary(n):
                    angles(1 if PHASES[n + 1][0] == "swa" else 0)
                if kind != "final":
                    squares_of_x(chunks=KC if n + 2 < len(PHASES) else 4)


_OUT = (1, T, D)


def kernel(**inputs):
    import numpy as _np
    import concourse.bacc as _bacc
    from concourse import mybir as _mybir
    from concourse.bass_utils import run_bass_kernel_spmd as _run

    a = {k: _np.ascontiguousarray(v) for k, v in inputs.items()}

    def by_feature(v):
        return v.reshape(-1, P).T

    cols = _np.concatenate([by_feature(v) for v in (
        a["norm_mix"], a["norm_mlp"], a["norm_final"], a["mla_q_norm"], a["mla_kv_norm"], a["lru_conv_w"],
        a["lru_conv_b"], a["lru_b_rgate"], a["lru_b_igate"], a["lru_lambda"], a["swa_b_in"][:, :1280],
        a["swa_b_o"])], axis=1)
    arrays = {
        "x": a["x"][0].T,
        "positions": a["positions"],
        "cols": cols,
        "const": rope_constants(),
        "swa_bv": a["swa_b_in"][:, 1280:],
        "swa_sinks": a["swa_sinks"],
    }
    for name in ("mla_w_in", "mla_w_uq", "mla_w_ukv", "mla_w_o", "lru_w_in", "lru_w_rgate", "lru_w_igate",
                 "lru_w_out", "swa_w_in", "swa_w_o", "mlp_w1", "mlp_w2"):
        arrays[name] = a[name]
    arrays = {f"in_{k}": _np.ascontiguousarray(v) for k, v in arrays.items()}

    nc = _bacc.Bacc("TRN2", target_bir_lowering=False, num_devices=1)
    A = {k[3:]: nc.dram_tensor(k, v.shape, _mybir.dt.from_np(v.dtype), kind="ExternalInput").ap()
         for k, v in arrays.items()}
    A["out"] = nc.dram_tensor("out", (D, T), _mybir.dt.float32, kind="ExternalOutput").ap()
    trunk(nc, A)
    r = _run(nc, [arrays], core_ids=[0])
    got = r.results[0]["out"]
    return _np.ascontiguousarray(got.T).reshape(_OUT)
```
